# Optimizing a Trainium2 kernel written in Bass

```python
import jax, jax.numpy as jnp
from jax import lax
import numpy as np

D_MODEL = 4096
BATCH = 1
SEQ = 256
DEPTH = 2

MIX_WIDTH = D_MODEL
BRANCH = MIX_WIDTH // 4

S5_GROUP = 16
S5_GROUPS = BRANCH // S5_GROUP
S5_STATE = 64
S5_DT_MIN = 1e-3
S5_DT_MAX = 1e-1

MLA_NOPE = 128
MLA_ROPE = 64
MLA_V = 128
MLA_HEADS = BRANCH // MLA_V
MLA_Q_RANK = D_MODEL * 3 // 16
MLA_KV_RANK = D_MODEL // 8
ROPE_THETA = 10000.0
Q_BLOCK = 128
NEG_INF = -1e30

GLA_HEADS = 4
GLA_DV = BRANCH // GLA_HEADS
GLA_DK = GLA_DV // 2
GLA_GATE_RANK = 16
GLA_TAU = 16.0
GLA_CHUNK = 64

LRU_BLOCKS = 8
LRU_BLOCK_W = BRANCH // LRU_BLOCKS
LRU_CONV = 4
LRU_C = 8.0

NORM_EPS = 1e-6

IN_SIZES = (BRANCH, BRANCH,
            MLA_Q_RANK, MLA_KV_RANK, MLA_ROPE, BRANCH,
            GLA_HEADS * GLA_DK, GLA_HEADS * GLA_DK, BRANCH,
            GLA_GATE_RANK, BRANCH,
            BRANCH, BRANCH)
IN_COLS = 7 * BRANCH + MLA_Q_RANK + MLA_KV_RANK + MLA_ROPE + 2 * GLA_HEADS * GLA_DK + GLA_GATE_RANK

kernel_name = "hybrid_s5_mla_gla_rglru_parallel_heads"

def rms_norm(x, g):
    x32 = x.astype(jnp.float32)
    y = x32 * lax.rsqrt(jnp.mean(x32 * x32, axis=-1, keepdims=True) + NORM_EPS)
    return (y * g.astype(jnp.float32)).astype(x.dtype)

def split_cols(z):
    idx = np.cumsum(IN_SIZES)[:-1].tolist()
    return jnp.split(z, idx, axis=-1)

def linear_scan(a, b):
    def combine(left, right):
        a_l, b_l = left
        a_r, b_r = right
        return a_l * a_r, a_r * b_l + b_r
    _, h = lax.associative_scan(combine, (a, b), axis=1)
    return h

def s5_mixer(u, lam_re, lam_im, b_re, b_im, c_re, c_im, d, log_dt, w_glu, b_glu):
    bsz, seq, _ = u.shape
    f32 = jnp.float32
    lam = lax.complex(lam_re.astype(f32), lam_im.astype(f32))
    dt = jnp.exp(log_dt.astype(f32))[:, None]
    lam_bar = jnp.exp(lam * dt)
    b_c = lax.complex(b_re.astype(f32), b_im.astype(f32))
    b_bar = ((lam_bar - 1.0) / lam)[..., None] * b_c
    c_c = lax.complex(c_re.astype(f32), c_im.astype(f32))
    ug = u.astype(f32).reshape(bsz, seq, S5_GROUPS, S5_GROUP)
    bu = jnp.einsum('blgh,gph->blgp', ug.astype(jnp.complex64), b_bar)
    state = linear_scan(jnp.broadcast_to(lam_bar, bu.shape), bu)
    y = jnp.einsum('blgp,ghp->blgh', state, c_c).real + d.astype(f32) * ug
    y = jax.nn.gelu(y.reshape(bsz, seq, BRANCH))
    y = y * jax.nn.sigmoid(y @ w_glu.astype(f32) + b_glu.astype(f32))
    return y.astype(u.dtype)

def rope(x, positions):
    half = MLA_ROPE // 2
    inv_freq = 1.0 / (ROPE_THETA ** (jnp.arange(half, dtype=jnp.float32) / half))
    ang = positions.astype(jnp.float32)[..., None] * inv_freq
    cos = jnp.cos(ang)[:, :, None, :]
    sin = jnp.sin(ang)[:, :, None, :]
    x32 = x.astype(jnp.float32)
    x1, x2 = x32[..., :half], x32[..., half:]
    return jnp.concatenate([x1 * cos - x2 * sin, x2 * cos + x1 * sin], axis=-1).astype(x.dtype)

def mla_mixer(c_q, c_kv, k_rope, positions, q_norm_g, kv_norm_g, w_uq, w_uk, w_uv):
    bsz, seq, _ = c_q.shape
    dqk = MLA_NOPE + MLA_ROPE
    q = (rms_norm(c_q, q_norm_g) @ w_uq).reshape(bsz, seq, MLA_HEADS, dqk)
    q = jnp.concatenate([q[..., :MLA_NOPE], rope(q[..., MLA_NOPE:], positions)], axis=-1)
    c = rms_norm(c_kv, kv_norm_g)
    k_nope = (c @ w_uk).reshape(bsz, seq, MLA_HEADS, MLA_NOPE)
    v = (c @ w_uv).reshape(bsz, seq, MLA_HEADS, MLA_V)
    k_r = rope(k_rope[:, :, None, :], positions)
    k = jnp.concatenate([k_nope, jnp.broadcast_to(k_r, (bsz, seq, MLA_HEADS, MLA_ROPE))], axis=-1)
    scale = dqk ** -0.5
    n_blk = seq // Q_BLOCK
    q_blocks = q.reshape(bsz, n_blk, Q_BLOCK, MLA_HEADS, dqk).transpose(1, 0, 2, 3, 4)
    key_idx = jnp.arange(seq)

    def attend(args):
        q_blk, blk = args
        s = jnp.einsum('bqhd,bkhd->bhqk', q_blk, k).astype(jnp.float32) * scale
        q_idx = blk * Q_BLOCK + jnp.arange(Q_BLOCK)
        s = jnp.where(key_idx[None, :] <= q_idx[:, None], s, NEG_INF)
        p = jax.nn.softmax(s, axis=-1).astype(v.dtype)
        return jnp.einsum('bhqk,bkhd->bqhd', p, v)

    o = lax.map(attend, (q_blocks, jnp.arange(n_blk)))
    return o.transpose(1, 0, 2, 3, 4).reshape(bsz, seq, MLA_HEADS * MLA_V)

def gla_mixer(q, k, v, g_lr, w_g2, b_g, out_g):
    bsz, seq, _ = q.shape
    n_ch = seq // GLA_CHUNK
    f32 = jnp.float32

    def chunks(t, dim):
        return t.astype(f32).reshape(bsz, n_ch, GLA_CHUNK, GLA_HEADS, dim).transpose(0, 3, 1, 2, 4)

    log_a = jax.nn.log_sigmoid(g_lr.astype(f32) @ w_g2.astype(f32) + b_g.astype(f32)) / GLA_TAU
    qc = chunks(q, GLA_DK) * GLA_DK ** -0.5
    kc = chunks(k, GLA_DK)
    vc = chunks(v, GLA_DV)
    cum = jnp.cumsum(chunks(log_a, GLA_DK), axis=3)
    q_dec = qc * jnp.exp(cum)
    k_inv = kc * jnp.exp(-cum)
    causal = jnp.tril(jnp.ones((GLA_CHUNK, GLA_CHUNK), dtype=bool))
    att = jnp.where(causal, jnp.einsum('bhncd,bhnsd->bhncs', q_dec, k_inv), 0.0)
    o = jnp.einsum('bhncs,bhnsv->bhncv', att, vc)
    total = cum[:, :, :, -1:, :]
    kv = jnp.einsum('bhncd,bhncv->bhndv', kc * jnp.exp(total - cum), vc)
    decay = jnp.exp(total[:, :, :, 0, :])

    def step(s, inp):
        dec, kv_n = inp
        return dec[..., None] * s + kv_n, s

    s0 = jnp.zeros((bsz, GLA_HEADS, GLA_DK, GLA_DV), f32)
    _, s_prev = lax.scan(step, s0, (jnp.moveaxis(decay, 2, 0), jnp.moveaxis(kv, 2, 0)))
    o = o + jnp.einsum('bhncd,bhndv->bhncv', q_dec, jnp.moveaxis(s_prev, 0, 2))
    o = o.transpose(0, 2, 3, 1, 4).reshape(bsz, seq, GLA_HEADS, GLA_DV)
    o = rms_norm(o, out_g.reshape(GLA_HEADS, GLA_DV))
    return o.reshape(bsz, seq, BRANCH).astype(q.dtype)

def rglru_mixer(x, conv_w, conv_b, w_a, b_a, w_x, b_x, lam):
    bsz, seq, _ = x.shape
    f32 = jnp.float32
    xc = lax.conv_general_dilated(
        x, conv_w.reshape(LRU_CONV, 1, BRANCH).astype(x.dtype), window_strides=(1,),
        padding=((LRU_CONV - 1, 0),), dimension_numbers=('NWC', 'WIO', 'NWC'),
        feature_group_count=BRANCH) + conv_b
    xb = xc.astype(f32).reshape(bsz, seq, LRU_BLOCKS, LRU_BLOCK_W)
    r = jax.nn.sigmoid(jnp.einsum('blhi,hij->blhj', xb, w_a.astype(f32))
                       + b_a.astype(f32).reshape(LRU_BLOCKS, LRU_BLOCK_W))
    i = jax.nn.sigmoid(jnp.einsum('blhi,hij->blhj', xb, w_x.astype(f32))
                       + b_x.astype(f32).reshape(LRU_BLOCKS, LRU_BLOCK_W))
    log_a = -LRU_C * r * jax.nn.softplus(-lam.astype(f32).reshape(LRU_BLOCKS, LRU_BLOCK_W))
    gated = jnp.sqrt(-jnp.expm1(2.0 * log_a)) * (i * xb)
    h = linear_scan(jnp.exp(log_a), gated)
    return h.reshape(bsz, seq, BRANCH).astype(x.dtype)

def setup_inputs(seed: int = 0) -> dict:
    key = jax.random.key(seed)
    ks = iter(jax.random.split(key, 48))
    f32 = jnp.float32
    L = DEPTH

    def nrm(shape, scale):
        return jax.random.normal(next(ks), shape, f32) * scale

    def gain(shape):
        return 1.0 + nrm(shape, 0.02)

    x = nrm((BATCH, SEQ, D_MODEL), 1.0)
    offset = jax.random.randint(next(ks), (BATCH, 1), 0, 4096, dtype=jnp.int32)
    positions = offset + jnp.arange(SEQ, dtype=jnp.int32)[None, :]
    norm_g = gain((L, D_MODEL))
    w_in = nrm((L, D_MODEL, IN_COLS), D_MODEL ** -0.5)
    n_idx = jnp.arange(S5_STATE, dtype=f32)
    s5_lambda_re = -0.5 + nrm((L, S5_GROUPS, S5_STATE), 0.01)
    s5_lambda_im = jnp.pi * n_idx + nrm((L, S5_GROUPS, S5_STATE), 0.01)
    s5_b_re = nrm((L, S5_GROUPS, S5_STATE, S5_GROUP), (2 * S5_GROUP) ** -0.5)
    s5_b_im = nrm((L, S5_GROUPS, S5_STATE, S5_GROUP), (2 * S5_GROUP) ** -0.5)
    s5_c_re = nrm((L, S5_GROUPS, S5_GROUP, S5_STATE), (2 * S5_STATE) ** -0.5)
    s5_c_im = nrm((L, S5_GROUPS, S5_GROUP, S5_STATE), (2 * S5_STATE) ** -0.5)
    s5_d = nrm((L, S5_GROUPS, S5_GROUP), 1.0)
    s5_log_dt = jax.random.uniform(next(ks), (L, S5_GROUPS), f32,
                                   float(np.log(S5_DT_MIN)), float(np.log(S5_DT_MAX)))
    s5_w_glu = nrm((L, BRANCH, BRANCH), BRANCH ** -0.5)
    s5_b_glu = nrm((L, BRANCH), 0.01)
    s5_out_g = gain((L, BRANCH))
    mla_q_norm_g = gain((L, MLA_Q_RANK))
    mla_kv_norm_g = gain((L, MLA_KV_RANK))
    mla_w_uq = nrm((L, MLA_Q_RANK, MLA_HEADS * (MLA_NOPE + MLA_ROPE)), MLA_Q_RANK ** -0.5)
    mla_w_uk = nrm((L, MLA_KV_RANK, MLA_HEADS * MLA_NOPE), MLA_KV_RANK ** -0.5)
    mla_w_uv = nrm((L, MLA_KV_RANK, MLA_HEADS * MLA_V), MLA_KV_RANK ** -0.5)
    mla_out_g = gain((L, BRANCH))
    gla_w_gate = nrm((L, GLA_GATE_RANK, GLA_HEADS * GLA_DK), GLA_GATE_RANK ** -0.5)
    gla_b_gate = nrm((L, GLA_HEADS * GLA_DK), 0.1)
    gla_out_g = gain((L, BRANCH))
    lru_conv_w = nrm((L, LRU_CONV, BRANCH), LRU_CONV ** -0.5)
    lru_conv_b = nrm((L, BRANCH), 0.01)
    lru_w_a = nrm((L, LRU_BLOCKS, LRU_BLOCK_W, LRU_BLOCK_W), LRU_BLOCK_W ** -0.5)
    lru_b_a = nrm((L, BRANCH), 0.01)
    lru_w_x = nrm((L, LRU_BLOCKS, LRU_BLOCK_W, LRU_BLOCK_W), LRU_BLOCK_W ** -0.5)
    lru_b_x = nrm((L, BRANCH), 0.01)
    a0 = jax.random.uniform(next(ks), (L, BRANCH), f32, 0.9, 0.999)
    p0 = a0 ** (1.0 / LRU_C)
    lru_lambda = jnp.log(p0) - jnp.log1p(-p0)
    lru_out_g = gain((L, BRANCH))
    w_out = nrm((L, MIX_WIDTH, D_MODEL), MIX_WIDTH ** -0.5)
    final_g = gain((D_MODEL,))
    return {"x": x, "positions": positions, "norm_g": norm_g, "w_in": w_in,
            "s5_lambda_re": s5_lambda_re, "s5_lambda_im": s5_lambda_im,
            "s5_b_re": s5_b_re, "s5_b_im": s5_b_im, "s5_c_re": s5_c_re, "s5_c_im": s5_c_im,
            "s5_d": s5_d, "s5_log_dt": s5_log_dt, "s5_w_glu": s5_w_glu, "s5_b_glu": s5_b_glu,
            "s5_out_g": s5_out_g, "mla_q_norm_g": mla_q_norm_g, "mla_kv_norm_g": mla_kv_norm_g,
            "mla_w_uq": mla_w_uq, "mla_w_uk": mla_w_uk, "mla_w_uv": mla_w_uv, "mla_out_g": mla_out_g,
            "gla_w_gate": gla_w_gate, "gla_b_gate": gla_b_gate, "gla_out_g": gla_out_g,
            "lru_conv_w": lru_conv_w, "lru_conv_b": lru_conv_b, "lru_w_a": lru_w_a, "lru_b_a": lru_b_a,
            "lru_w_x": lru_w_x, "lru_b_x": lru_b_x, "lru_lambda": lru_lambda, "lru_out_g": lru_out_g,
            "w_out": w_out, "final_g": final_g}

def reference(x, positions, norm_g, w_in, s5_lambda_re, s5_lambda_im, s5_b_re, s5_b_im,
              s5_c_re, s5_c_im, s5_d, s5_log_dt, s5_w_glu, s5_b_glu, s5_out_g,
              mla_q_norm_g, mla_kv_norm_g, mla_w_uq, mla_w_uk, mla_w_uv, mla_out_g,
              gla_w_gate, gla_b_gate, gla_out_g, lru_conv_w, lru_conv_b, lru_w_a, lru_b_a,
              lru_w_x, lru_b_x, lru_lambda, lru_out_g, w_out, final_g):
    for l in range(DEPTH):
        h = rms_norm(x, norm_g[l])
        z = h @ w_in[l]
        (s5_u, s5_gate, mla_cq, mla_ckv, mla_kr, mla_gate, gla_q, gla_k, gla_v,
         gla_glr, gla_gate, lru_u, lru_gate) = split_cols(z)
        y_s5 = rms_norm(s5_mixer(s5_u, s5_lambda_re[l], s5_lambda_im[l], s5_b_re[l], s5_b_im[l],
                                 s5_c_re[l], s5_c_im[l], s5_d[l], s5_log_dt[l], s5_w_glu[l],
                                 s5_b_glu[l]), s5_out_g[l]) * jax.nn.silu(s5_gate)
        y_mla = rms_norm(mla_mixer(mla_cq, mla_ckv, mla_kr, positions, mla_q_norm_g[l],
                                   mla_kv_norm_g[l], mla_w_uq[l], mla_w_uk[l], mla_w_uv[l]),
                         mla_out_g[l]) * jax.nn.silu(mla_gate)
        y_gla = gla_mixer(gla_q, gla_k, gla_v, gla_glr, gla_w_gate[l], gla_b_gate[l],
                          gla_out_g[l]) * jax.nn.silu(gla_gate)
        y_lru = rms_norm(rglru_mixer(lru_u, lru_conv_w[l], lru_conv_b[l], lru_w_a[l], lru_b_a[l],
                                     lru_w_x[l], lru_b_x[l], lru_lambda[l]),
                         lru_out_g[l]) * jax.nn.silu(lru_gate)
        y = jnp.concatenate([y_s5, y_mla, y_gla, y_lru], axis=-1)
        x = x + y @ w_out[l]
    return rms_norm(x, final_g)


_drawn_inputs = setup_inputs


def setup_inputs(seed=0):
    import zlib

    import numpy as np

    out = dict(_drawn_inputs(seed))
    spreads = {}
    factors = {'s5_lambda_re': 8.0,
     's5_lambda_im': 2.699,
     's5_b_re': 3.827,
     's5_b_im': 3.781,
     's5_c_re': 3.872,
     's5_c_im': 3.802,
     's5_log_dt': 2.727,
     's5_b_glu': 8.0,
     's5_out_g': 7.333,
     'mla_q_norm_g': 8.0,
     'mla_kv_norm_g': 5.829,
     'mla_out_g': 7.434,
     'gla_b_gate': 3.59,
     'gla_out_g': 7.608,
     'lru_b_a': 8.0,
     'lru_b_x': 8.0,
     'lru_out_g': 7.476,
     'final_g': 2.814}
    for name, (base, spread) in spreads.items():
        noise = np.random.default_rng([zlib.crc32(name.encode()), seed]).standard_normal(out[name].shape)
        drawn = base * np.exp(spread * noise) if base else spread * noise
        out[name] = __import__('jax').numpy.asarray(drawn.astype(out[name].dtype))
    for name, factor in factors.items():
        out[name] = (out[name] * factor).astype(out[name].dtype)
    return out
```

```python
import numpy as np
import concourse.bass as bass
from concourse import mybir
from contextlib import ExitStack

P = 128
L = 2
T = 256
D = 4096
KT = D // P
BR = D // 4
G8 = BR // P
QR, KVR, ROPE = D * 3 // 16, D // 8, 64
CQ, CKV = QR // P, KVR // P
CC = 256
CH_HALF = KT // 2
CH_PAIR = 2 * CH_HALF
CH_GLU = 4
N_PRE, N_V, N_GATE = 0, 9 * CH_PAIR, 11 * CH_PAIR
N_GLU = N_GATE + G8 * CH_PAIR
N_OUT = N_GLU + 4 * CH_GLU
N_LAYER = N_OUT + 8 * CH_PAIR
H_PRE, H_V, H_GATE = 0, 18, 22
H_GLU = H_GATE + 2 * G8
H_OUT = H_GLU + 4
H_LAYER = H_OUT + 16
RAW, W2, LOOK = 8, 4, 3
Z_LRU, Z_S5, Z_Q, Z_K, Z_CQ, Z_CKV = 0, 8, 16, 20, 24, 30
NZ = 34
(C_CONV, C_CONVB, C_BA, C_BX, C_LAM, C_LRUG, C_MLAG, C_GLAG, C_GLAB, C_S5D) = (0, 4, 5, 6, 7, 8, 9, 10, 11, 12)
C_SP2, C_HBA, C_HBX, C_F0, C_R, C_SR, C_NSI, NPG = 13, 14, 15, 16, 20, 24, 28, 32
NPG_IN = 13
K_PERM1, K_PERM2, K_ID, K_AMASK, K_GMASK, K_CMASK, K_IOTA, K_INVF, NK = 0, 128, 256, 384, 640, 768, 1024, 1280, 1281
S_NORM, S_QG, S_KVG, S_BGLU, S_S5G, S_FG, NS = 0, 32, 38, 42, 50, 58, 90
EPS = 1e-6
MAGIC = 12582912.0
TWO_PI = 6.283185
SCALE = float(128 + ROPE) ** -0.5
TAU = 16.0
HEAVY = 1.0e30


def trunk(nc, w, x, pos, const, small, pg_in, s5raw, mlaw_d, mixw_d, wg2_d, out):
    F, R, I = mybir.dt.float32, mybir.dt.float32r, mybir.dt.int32
    ACT, ALU, AX = mybir.ActivationFunctionType, mybir.AluOpType, mybir.AxisListType
    ctx = ExitStack()
    with ctx:
        def sb(name, shape, dt=F):
            return ctx.enter_context(nc.sbuf_tensor(name, shape, dt))

        def sem(name):
            return ctx.enter_context(nc.semaphore(name))

        xres = nc.dram_tensor("xres", (P, KT, T), F).ap()

        hb = sb("hb", [P, KT, 2, T], R)
        raw = sb("raw", [P, RAW, 2, CC])
        w2 = sb("w2", [P, W2, 2, 2, CC], R)
        zb = sb("zb", [P, NZ, T])
        kg = sb("kg", [P, T])
        vb = sb("vb", [P, G8, 2, P])
        ymla = sb("ymla", [P, G8, T])
        gs5 = sb("gs5", [P, G8, T])
        half_lo = sb("half_lo", [P, 2, T])
        gate = sb("gate", [P, 2, 2, T])
        kc = sb("kc", [P, NK])
        sm_all = sb("sm_all", [P, L, NS])
        sm = sb("sm", [P, NS])
        pg_all = sb("pg_all", [P, L, G8, NPG_IN])
        pgl = sb("pgl", [P, G8, NPG])
        pg = sb("pg", [P, NPG])
        cst = sb("cst", [P, 4])
        ones = sb("ones", [P, 1])
        rope = sb("rope", [P, T])
        kext = sb("kext", [P, T])
        mlaw = sb("mlaw", [P, CQ * T])
        mixw = sb("mixw", [P, 6, P])
        wg2 = sb("wg2", [P, P])
        cprime = sb("cprime", [P, 2, 4, 32])
        xx = sb("xx", [P, 2, T])
        yy = sb("yy", [P, 2, T])
        g2 = sb("g2", [P, 2, T])
        tab = sb("tab", [P, 4, T])
        nf = sb("nf", [P, T])
        tau = sb("tau", [P, T])
        us = sb("us", [P, T])
        yl = sb("yl", [P, T])
        kv = sb("kv", [P, 2, T])
        prob = sb("prob", [P, 3, P])
        probt = sb("probt", [P, 3, P])
        ym = sb("ym", [P, T])
        row = sb("row", [P, 8])
        ga = sb("ga", [P, T])
        gb = sb("gb", [P, T])
        lg = sb("lg", [P, 2, T])
        qd = sb("qd", [P, T])
        ki = sb("ki", [P, T])
        ke = sb("ke", [P, T])
        attm = sb("attm", [P, 2, P])
        st = sb("st", [P, 3, P])
        tot = sb("tot", [P, 4])
        vs = sb("vs", [P, 2, P])
        yg = sb("yg", [P, T])
        xc = probt[:, 0:2, :].rearrange("p a t -> p (a t)")
        trti = lg[:, :, :]
        cum, ep = lg[:, 0, :], lg[:, 1, :]
        tw, sq = qd[:, :], yg[:, :]
        qn = st[:, 0:2, :].rearrange("p a t -> p (a t)")
        qr = prob[:, 0:2, :].rearrange("p a t -> p (a t)")
        posi = kext[:, :].bitcast(I)
        sqp = sb("sqp", [P, T])
        ssq = sb("ssq", [P, 6, T])
        sx = sb("sx", [P, T])
        ncol = sb("ncol", [P, 12])
        rcol = sb("rcol", [P, 12])
        s5_all = sb("s5_all", [P, L, 3, 32])
        s5 = gate[:, :, :, :].rearrange("p h a (r b) -> p (h a r) b", b=32)
        lru8 = sb("lru8", [P, 6, G8])
        hf = (xx, yy)

        ps = ctx.enter_context(nc.psum_tensor("ps", [P, 8, 512], F))
        B_BU, B_Y, B_A, B_B = 4, 5, 6, 7

        x_loaded = [sem(f"x_loaded{i}") for i in range(8)]
        const_loaded, pos_loaded, small_loaded = sem("const_loaded"), sem("pos_loaded"), sem("small_loaded")
        raw_loaded = [sem(f"raw_loaded{i}") for i in range(RAW)]
        qw_loaded, kvw_loaded, mix_loaded, wg2_loaded = (sem("qw_loaded"), sem("kvw_loaded"), sem("mix_loaded"),
                                                        sem("wg2_loaded"))
        xold_loaded, x_stored, out_stored = [sem("xold_loaded0"), sem("xold_loaded1")], sem("x_stored"), sem("out_stored")
        hi_ready, w2_ready, chunk_done = sem("hi_ready"), sem("w2_ready"), sem("chunk_done")
        lo_copied, acc_read = sem("lo_copied"), sem("acc_read")
        squares_made, sx_ready, x_ready = sem("squares_made"), sem("sx_ready"), sem("x_ready")
        hf_ready, h_hi_ready, h_ready = sem("hf_ready"), sem("h_hi_ready"), sem("h_ready")
        cols_ready, rms_ready, rcol_ready, rstd_ready = (sem("cols_ready"), sem("rms_ready"), sem("rcol_ready"),
                                                         sem("rstd_ready"))
        rope_made, consts_made = sem("rope_made"), sem("consts_made")
        kperm_ready, krot_ready, ksum_ready, kext_ready = (sem("kperm_ready"), sem("krot_ready"), sem("ksum_ready"),
                                                           sem("kext_ready"))
        latent_squared, latents_ready, ssq_cleared = sem("latent_squared"), sem("latents_ready"), sem("ssq_cleared")
        pgl_dve, pgl_act, act_prep, dve_prep = sem("pgl_dve"), sem("pgl_act"), sem("act_prep"), sem("dve_prep")
        iter_done, pg_ready, us_ready, vs_ready = sem("iter_done"), sem("pg_ready"), sem("us_ready"), sem("vs_ready")
        cprime_ready, nf_ready, tab_ready = sem("cprime_ready"), sem("nf_ready"), sem("tab_ready")
        bu_ready, bu_read, tab_used, state_ready, state_used = (sem("bu_ready"), sem("bu_read"), sem("tab_used"),
                                                                sem("state_ready"), sem("state_used"))
        xc_ready, ri_ready, lru_act, yl_ready, yl_squared = (sem("xc_ready"), sem("ri_ready"), sem("lru_act"),
                                                             sem("yl_ready"), sem("yl_squared"))
        q_ready, qn_ready, qr_ready, kv_ready, kv_copied = (sem("q_ready"), sem("qn_ready"), sem("qr_ready"),
                                                            sem("kv_ready"), sem("kv_copied"))
        sc_ready, sc_read, max_ready, prob_ready, probn_ready = (sem("sc_ready"), sem("sc_read"), sem("max_ready"),
                                                                 sem("prob_ready"), sem("probn_ready"))
        pt_ready, pt_copied, o_ready, ym_ready, ym_squared = (sem("pt_ready"), sem("pt_copied"), sem("o_ready"),
                                                              sem("ym_ready"), sem("ym_squared"))
        la_ready, la_abs, la_act, cum_ready, decays_ready = (sem("la_ready"), sem("la_abs"), sem("la_act"),
                                                             sem("cum_ready"), sem("decays_ready"))
        qk_ready, att_ready, ket_copied, att_masked = (sem("qk_ready"), sem("att_ready"), sem("ket_copied"),
                                                       sem("att_masked"))
        kvs_ready, st_ready, og_ready, yg_ready, yg_squared = (sem("kvs_ready"), sem("st_ready"), sem("og_ready"),
                                                               sem("yg_ready"), sem("yg_squared"))
        silu_ready, glu_hi, glu_ready, glu_tanh, glu_squared, y2_ready = (
            sem("silu_ready"), sem("glu_hi"), sem("glu_ready"), sem("glu_tanh"), sem("glu_squared"), sem("y2_ready"))
        sx_first = sem("sx_first")
        gelu_done, outx_ready, outx, gla_exp = sem("gelu_done"), sem("outx_ready"), sem("outx"), sem("gla_exp")
        act_own, dve_own, pool_own = sem("act_own"), sem("dve_own"), sem("pool_own")
        block = ctx.enter_context(nc.Block())

        class Own:

            def __init__(self, eng, s):
                self.eng, self.s, self.n = eng, s, 0

            def do(self, ins):
                ins.then_inc(self.s, 1)
                self.n += 1

            def wait(self):
                self.eng.wait_ge(self.s, self.n)

            def chain(self, ins):
                self.do(ins)
                self.wait()

            def pause(self):
                self.eng.sem_inc(self.s, 1)
                self.n += 1

            def restart(self):
                if self.n:
                    self.pause()
                    self.wait()
                    self.eng.sem_clear(self.s)
                    self.n = 0

        @block.sync
        def _(sp):
            for i in range(8):
                sp.dma_start(zb[:, 4 * i:4 * i + 4, :], x[:, 4 * i:4 * i + 4, :]).then_inc(x_loaded[i], 16)
            for s in range(RAW):
                sp.dma_start(raw[:, s], w[s]).then_inc(raw_loaded[s], 16)
            with sp.Fori(0, L * N_LAYER // RAW - 1) as q:
                for s in range(RAW):
                    sp.wait_ge(w2_ready, q * RAW + s + 1)
                    sp.dma_start(raw[:, s], w[q * RAW + (RAW + s)]).then_inc(raw_loaded[s], 16)
            for s in range(LOOK):
                sp.wait_ge(w2_ready, L * N_LAYER - RAW + s + 1)
                sp.dma_start(raw[:, s], w[s]).then_inc(raw_loaded[s], 16)
            for i in range(4):
                sp.wait_ge(outx_ready, i + 1)
                sp.dma_start(out[:, 8 * i:8 * i + 8, :], zb[:, 8 * i:8 * i + 8, :]).then_inc(out_stored, 16)
            sp.wait_ge(out_stored, 64)
            sp.wait_ge(x_stored, 16 * (1 + 16 * L))

        @block.tensor
        def _(pe):
            mm = nc.tensor.matmul

            def chunk(n0, c, half, tokens=False, tiles=(0, 1), k0=0, nk=KT):
                kcs = 2 * (c % (nk // 2))
                pe.wait_ge(w2_ready, n0 + (c + 1))
                for kk in range(2):
                    k = kcs + kk
                    for j in tiles:
                        acc = ps[:, 2 * half + j, :]
                        s = c % W2
                        if tokens:
                            a_hi, a_lo = hb[:, k0 + k, 0, P * j:P * j + P], hb[:, k0 + k, 1, P * j:P * j + P]
                            m_both, m_hi = w2[:, s, kk, :, :].rearrange("p a c -> p (a c)"), w2[:, s, kk, 0, :]
                        else:
                            a_hi, a_lo = w2[:, s, kk, 0, P * j:P * j + P], w2[:, s, kk, 1, P * j:P * j + P]
                            m_both, m_hi = hb[:, k0 + k, :, :].rearrange("p a c -> p (a c)"), hb[:, k0 + k, 0, :]
                        if k > 0:
                            mm(acc[:, T:], a_lo, m_hi, start=False, stop=False, skip_group_check=True)
                        last = mm(acc, a_hi, m_both, start=(k == 0), stop=(k == nk - 1), skip_group_check=True)
                        if k == 0:
                            last = mm(acc[:, T:], a_lo, m_hi, start=False, stop=False, skip_group_check=True)
                last.then_inc(chunk_done, 1)

            def columns(srcs, count):
                for i, s in enumerate(srcs):
                    for b in range(2):
                        last = mm(ps[:, B_Y, 2 * i + b:2 * i + b + 1], s[:, P * b:P * b + P], ones[:, :],
                                  start=True, stop=True)
                last.then_inc(cols_ready, 1)

            def spread(dsts, count):
                pe.wait_ge(rcol_ready, count)
                for i, d in enumerate(dsts):
                    for b in range(2):
                        last = mm(d[:, P * b:P * b + P], rcol[:, 2 * i + b:2 * i + b + 1].to_broadcast([P, P]),
                                  kc[:, K_ID:K_ID + P], start=True, stop=True)
                last.then_inc(rstd_ready, 1)

            pe.sem_inc(chunk_done, W2)
            pe.sem_inc(state_used, 1)
            pe.wait_ge(const_loaded, 16)
            pe.wait_ge(consts_made, 1)

            with pe.Fori(0, L) as l:
                n_l, h_l, c_l = l * N_LAYER, l * H_LAYER, l * 4
                pe.wait_ge(sx_ready, l + 1)
                columns([sx], None)
                spread([ps[:, B_BU, 0:T]], c_l + 1)
                for c in range(CH_PAIR):
                    if c % CH_HALF == 0:
                        pe.wait_ge(acc_read, h_l + c // CH_HALF + 1)
                    if c < CH_HALF:
                        pe.wait_ge(h_ready, l * 32 + (c + 1))
                    chunk(n_l, c, c // CH_HALF)
                with pe.Fori(1, 8) as i:
                    n0, h0 = n_l + i * CH_PAIR, h_l + i * 2
                    for c in range(CH_PAIR):
                        if c % CH_HALF == 0:
                            pe.wait_ge(acc_read, h0 + (c // CH_HALF + 1))
                        chunk(n0, c, c // CH_HALF)
                for c in range(CH_PAIR):
                    if c % CH_HALF == 0:
                        pe.wait_ge(acc_read, h_l + (16 + c // CH_HALF + 1))
                    chunk(n_l + 8 * CH_PAIR, c, c // CH_HALF, tiles=(0, 1) if c < CH_HALF else (0,))
                for c in range(2 * CH_PAIR):
                    if c % CH_HALF == 0:
                        pe.wait_ge(acc_read, h_l + (H_V + c // CH_HALF + 1))
                    chunk(n_l + N_V, c, (c // CH_HALF) % 2, tokens=True)
                    if c == 3:
                        pe.wait_ge(acc_read, h_l + H_V + 2)
                        mm(ps[:, B_A, 0:T], kc[0:ROPE, K_PERM1:K_PERM1 + P], kg[0:ROPE, :], start=True,
                           stop=True).then_inc(kperm_ready, 1)
                    if c == 6:
                        pe.wait_ge(krot_ready, l + 1)
                        mm(ps[:, B_A, 0:T], kc[:, K_PERM2:K_PERM2 + P], qr[:, :], start=True,
                           stop=True).then_inc(ksum_ready, 1)
                    if c == 20:
                        pe.wait_ge(latent_squared, 10 * l + 10)
                        columns([ssq[:, 2, :], ssq[:, 3, :]], None)
                    if c == 23:
                        spread([ps[:, B_B, 0:T], ps[:, B_B, T:]], c_l + 2)

                with pe.Fori(0, G8) as g:
                    it = l * G8 + g
                    n0, h0 = n_l + N_GATE + g * CH_PAIR, h_l + H_GATE + g * 2

                    def s5_in(j):
                        if j == 0:
                            pe.wait_ge(us_ready, it + 1)
                            pe.wait_ge(mix_loaded, it * 16 + 16)
                        pe.wait_ge(bu_read, it * 4 + (j + 1))
                        r = slice(32 * j, 32 * j + 32)
                        mm(ps[:, B_BU, 0:T], mixw[r, 2, :], us[r, :], start=True, stop=True)
                        mm(ps[:, B_BU, T:], mixw[r, 3, :], us[r, :], start=True, stop=True).then_inc(bu_ready, 1)

                    def s5_out(j):
                        if j == 0:
                            pe.wait_ge(cprime_ready, it + 1)
                            pe.wait_ge(iter_done, it + 1)
                        pe.wait_ge(state_ready, it * 4 + (j + 1))
                        o = ps[32 * j:32 * j + 32, B_Y, 0:T]
                        mm(o, cprime[:, 0, j, :], xx[:, 0, :], start=True, stop=False)
                        mm(o, cprime[:, 1, j, :], xx[:, 1, :], start=False, stop=True).then_inc(state_used, 1)

                    def lru_gates():
                        pe.wait_ge(xc_ready, it + 1)
                        pe.wait_ge(st_ready, it + 1)
                        mm(ps[:, B_B, 0:T], mixw[:, 0, :], xc[:, :], start=True, stop=True)
                        mm(ps[:, B_B, T:], mixw[:, 1, :], xc[:, :], start=True, stop=True).then_inc(ri_ready, 1)

                    def mla_q():
                        pe.wait_ge(qw_loaded, it * 16 + 16)
                        pe.wait_ge(latents_ready, 10 * l + 10)
                        pe.wait_ge(yg_ready, it + 1)
                        for part in range(2):
                            for k in range(CQ):
                                last = mm(ps[:, B_A, T * part:T * part + T],
                                          mlaw[:, T * k + P * part:T * k + P * part + P], zb[:, Z_CQ + k, :],
                                          start=(k == 0), stop=(k == CQ - 1))
                        last.then_inc(q_ready, 1)

                    def mla_kv():
                        pe.wait_ge(kvw_loaded, it * 16 + 16)
                        pe.wait_ge(qr_ready, it + 1)
                        for k in range(CKV):
                            mm(ps[:, B_A, 0:T], mlaw[:, P * k:P * k + P], zb[:, Z_CKV + k, :],
                               start=(k == 0), stop=(k == CKV - 1))
                        for b in range(2):
                            for k in range(CKV):
                                last = mm(ps[:, B_A, T + P * b:T + P * b + P], zb[:, Z_CKV + k, P * b:P * b + P],
                                          mlaw[:, KVR + P * k:KVR + P * k + P], start=(k == 0), stop=(k == CKV - 1))
                        last.then_inc(kv_ready, 1)

                    def mla_scores():
                        pe.wait_ge(kv_copied, it + 1)
                        for b in range(2):
                            o = ps[:, B_A, P * b:P * b + P * (b + 1)]
                            mm(o, qn[:, P * b:P * b + P], kv[:, 0, 0:P * (b + 1)], start=True, stop=False)
                            last = mm(o, qr[:, P * b:P * b + P], kext[:, 0:P * (b + 1)], start=False, stop=True)
                        last.then_inc(sc_ready, 1)

                    def mla_turn():
                        pe.wait_ge(probn_ready, it + 1)
                        for b in range(3):
                            last = nc.tensor.transpose(ps[:, B_A, P * b:P * b + P], prob[:, b, :], kc[:, K_ID:K_ID + P])
                        last.then_inc(pt_ready, 1)

                    def mla_out():
                        pe.wait_ge(pt_copied, it + 1)
                        mm(ps[:, B_A, 0:P], kv[:, 1, 0:P], probt[:, 0, :], start=True, stop=True)
                        mm(ps[:, B_A, P:T], kv[:, 1, 0:P], probt[:, 1, :], start=True, stop=False)
                        mm(ps[:, B_A, P:T], kv[:, 1, P:T], probt[:, 2, :], start=False, stop=True).then_inc(o_ready, 1)

                    def gla_gate():
                        pe.wait_ge(wg2_loaded, it * 16 + 16)
                        pe.wait_ge(lru_act, it + 2)
                        mm(ps[:, B_B, 0:T], wg2[64:80, :], kg[64:80, :], start=True, stop=True).then_inc(la_ready, 1)

                    def gla_scores():
                        pe.wait_ge(qk_ready, it + 1)
                        pe.wait_ge(ym_ready, it + 2)
                        for b in range(2):
                            mm(ps[:, B_A, P * b:P * b + P], ki[:, P * b:P * b + P], qd[:, P * b:P * b + P],
                               start=True, stop=True)
                        for b in range(2):
                            last = nc.tensor.transpose(ps[:, B_A, T + P * b:T + P * b + P], ke[:, P * b:P * b + P],
                                                       kc[:, K_ID:K_ID + P])
                        last.then_inc(att_ready, 1)

                    def gla_states():
                        pe.wait_ge(ket_copied, it + 1)
                        pe.wait_ge(cum_ready, it + 1)
                        pe.wait_ge(vs_ready, it + 1)
                        for c in (0, 2, 1):
                            if c == 1:
                                pe.wait_ge(kvs_ready, it * 2 + 1)
                            r = slice(64 * (c % 2), 64 * (c % 2) + 64)
                            last = mm(ps[:, B_B, P * c:P * c + P], probt[r, c // 2, :], vs[r, c // 2, :],
                                      start=True, stop=True)
                            if c:
                                last.then_inc(kvs_ready, 1)

                    def gla_out():
                        pe.wait_ge(att_masked, it + 1)
                        pe.wait_ge(st_ready, it + 2)
                        for c in range(4):
                            r, a = slice(64 * c, 64 * c + 64), slice(64 * (c % 2), 64 * (c % 2) + 64)
                            last = mm(ps[:, B_A, r], vs[:, c // 2, :], attm[:, c // 2, a], start=True, stop=(c == 0))
                            if c:
                                last = mm(ps[:, B_A, r], st[:, c - 1, :], qd[:, r], start=False, stop=True)
                        last.then_inc(og_ready, 1)

                    steps = {0: [mla_q], 1: [lambda: s5_in(0)], 2: [lru_gates], 5: [mla_kv],
                             6: [gla_gate], 7: [mla_scores, lambda: s5_in(1)], 8: [lambda: s5_out(0)],
                             12: [mla_turn], 14: [mla_out], 15: [lambda: s5_out(1), lambda: s5_in(2)],
                             23: [lambda: s5_out(2), lambda: s5_in(3)], 24: [gla_scores], 26: [gla_states],
                             29: [gla_out], 31: [lambda: s5_out(3)]}
                    for c in range(CH_PAIR):
                        if c % CH_HALF == 0:
                            pe.wait_ge(acc_read, h0 + (c // CH_HALF + 1))
                        chunk(n0, c, c // CH_HALF)
                        for step in steps.get(c, ()):
                            step()

                pe.wait_ge(iter_done, l * G8 + (G8 + 1))
                pe.wait_ge(yg_squared, l * G8 + G8)
                columns([ssq[:, i, :] for i in range(6)], None)
                for c in range(4 * CH_GLU):
                    if c % CH_GLU == 0:
                        pe.wait_ge(acc_read, h_l + (H_GLU + c // CH_GLU + 1))
                    if c < CH_GLU:
                        pe.wait_ge(glu_ready, l * 4 + (c + 1))
                    if c == 2:
                        spread([ps[:, B_BU, 0:T], ps[:, B_BU, T:], ps[:, B_A, 0:T], ps[:, B_A, T:],
                                ps[:, B_B, 0:T], ps[:, B_B, T:]], c_l + 3)
                    chunk(n_l + N_GLU, c, (c // CH_GLU) % 2, k0=24, nk=8)
                for c in range(CH_PAIR):
                    if c % CH_HALF == 0:
                        pe.wait_ge(acc_read, h_l + (H_OUT + c // CH_HALF + 1))
                    if c == 5:
                        pe.wait_ge(glu_squared, l * 4 + 4)
                        columns([sx], None)
                    if c == 8:
                        spread([ps[:, B_Y, 0:T]], c_l + 4)
                    if c < CH_HALF:
                        pe.wait_ge(h_ready, l * 32 + (16 + c + 1))
                    chunk(n_l + N_OUT, c, c // CH_HALF)
                with pe.Fori(1, 8) as i:
                    n0, h0 = n_l + N_OUT + i * CH_PAIR, h_l + H_OUT + i * 2
                    for c in range(CH_PAIR):
                        if c % CH_HALF == 0:
                            pe.wait_ge(acc_read, h0 + (c // CH_HALF + 1))
                        chunk(n0, c, c // CH_HALF)
            pe.wait_ge(sx_ready, L + 1)
            columns([sx], None)
            spread([ps[:, B_BU, 0:T]], 4 * L + 1)

        @block.scalar
        def _(act):
            own = Own(act, act_own)
            A = nc.scalar.activation
            EPS1, EPS4, HALF_PI, ONE = cst[:, 0:1], cst[:, 1:2], cst[:, 2:3], cst[:, 3:4]

            def hi(n0, c):
                s, d = (c + LOOK) % RAW, (c + LOOK) % W2
                act.wait_ge(raw_loaded[s], n0 * (16 // RAW) + 16 * ((c + LOOK) // RAW + 1))
                act.wait_ge(chunk_done, n0 + (c + LOOK + 1))
                A(w2[:, d, :, 0, :], raw[:, s, :, :], ACT.Copy).then_inc(hi_ready, 1)

            def evac(h0, half, n_done, tiles=2):
                act.wait_ge(chunk_done, n_done + W2)
                act.wait_ge(acc_read, h0 + 2)
                A(half_lo[:, 0:tiles, :], ps[:, 2 * half:2 * half + tiles, 0:T], ACT.Copy).then_inc(lo_copied, 1)

            def rms(count, cols, n, eps):
                act.wait_ge(cols_ready, count)
                A(ncol[:, 0:cols], ps[:, B_Y, 0:cols], ACT.Sqrt, bias=eps, scale=1.0 / n).then_inc(rms_ready, 1)

            def split_hi(k, count):
                act.wait_ge(hf_ready, count)
                A(hb[:, 2 * k:2 * k + 2, 0, :], hf[k % 2][:, :, :], ACT.Copy).then_inc(h_hi_ready, 1)

            act.dma_start(kc[:, :], const).then_inc(const_loaded, 16)
            act.dma_start(posi[:, :], pos.partition_broadcast(P)).then_inc(pos_loaded, 16)
            act.dma_start(sm_all[:, :, :], small).then_inc(small_loaded, 16)
            act.dma_start(pg_all[:, :, :, :], pg_in).then_inc(small_loaded, 16)
            act.dma_start(s5_all[:, :, :, :], s5raw).then_inc(small_loaded, 16)
            act.dma_start(mlaw[:, :], mlaw_d[0, :, 0:CQ * T]).then_inc(qw_loaded, 16)
            act.dma_start(mixw[:, :, :], mixw_d[0]).then_inc(mix_loaded, 16)
            act.dma_start(wg2[64:80, :], wg2_d[0]).then_inc(wg2_loaded, 16)
            for i in range(8):
                act.wait_ge(x_loaded[i], 16)
                if i >= 2:
                    act.wait_ge(x_ready, i - 1)
                A(gs5[:, 4 * (i % 2):4 * (i % 2) + 4, :], zb[:, 4 * i:4 * i + 4, :], ACT.Square).then_inc(squares_made, 1)
            act.dma_start(xres, zb[:, 0:KT, :]).then_inc(x_stored, 16)
            for s in range(LOOK):
                act.wait_ge(raw_loaded[s], 16)
                act.wait_ge(chunk_done, s + 1)
                A(w2[:, s, :, 0, :], raw[:, s, :, :], ACT.Copy).then_inc(hi_ready, 1)
            act.wait_ge(consts_made, 1)
            act.wait_ge(rope_made, 1)
            A(gb[0:64, :], ga[0:64, :], ACT.Abs).then_inc(act_prep, 1)
            act.wait_ge(act_prep, 1)
            A(rope[0:64, :], gb[0:64, :], ACT.Sin, bias=HALF_PI[0:64], scale=-1.0).then_inc(act_prep, 1)
            A(rope[64:96, :], ga[64:96, :], ACT.Sin, scale=-1.0).then_inc(act_prep, 1)
            A(rope[96:128, :], ga[96:128, :], ACT.Sin).then_inc(act_prep, 1)
            act.sem_inc(yg_ready, 1)
            act.sem_inc(ym_ready, 1)
            act.sem_inc(lru_act, 1)
            act.sem_inc(tab_ready, 1)

            with act.Fori(0, L) as l:
                n_l, h_l, c_l = l * N_LAYER, l * H_LAYER, l * 4
                rms(c_l + 1, 2, D, EPS1)
                for c in range(CH_PAIR):
                    if c < CH_HALF:
                        split_hi(c, l * 32 + (c + 1))
                    hi(n_l, c)
                    if c % CH_HALF == CH_HALF - 1:
                        evac(h_l + c // CH_HALF, c // CH_HALF, n_l + (c + 1))
                with act.Fori(1, 8) as i:
                    n0, h0 = n_l + i * CH_PAIR, h_l + i * 2
                    for c in range(CH_PAIR):
                        hi(n0, c)
                        if c % CH_HALF == CH_HALF - 1:
                            evac(h0 + c // CH_HALF, c // CH_HALF, n0 + (c + 1))
                for c in range(CH_PAIR):
                    hi(n_l + 8 * CH_PAIR, c)
                    if c % CH_HALF == CH_HALF - 1:
                        evac(h_l + (16 + c // CH_HALF), c // CH_HALF, n_l + (8 * CH_PAIR + c + 1), 2 - c // CH_HALF)
                for c in range(2 * CH_PAIR):
                    hi(n_l + N_V, c)
                    if c % CH_HALF == CH_HALF - 1:
                        evac(h_l + (H_V + c // CH_HALF), (c // CH_HALF) % 2, n_l + (N_V + c + 1))
                    if c == 21:
                        act.wait_ge(cols_ready, c_l + 2)
                        A(ncol[:, 0:2], ps[:, B_Y, 0:2], ACT.Sqrt, bias=EPS1, scale=1.0 / QR)
                        A(ncol[:, 2:4], ps[:, B_Y, 2:4], ACT.Sqrt, bias=EPS1, scale=1.0 / KVR).then_inc(rms_ready, 1)
                    if c == 10:
                        act.wait_ge(pgl_dve, 3 * l + 1)
                        A(lru8[:, 1, :], lru8[:, 0, :], ACT.Exp, scale=-1.0).then_inc(pgl_act, 1)
                    if c == 34:
                        act.wait_ge(pgl_dve, 3 * l + 3)
                        A(s5[:, 8, :], s5[:, 7, :], ACT.Sin, scale=TWO_PI)
                        A(s5[:, 9, :], s5[:, 7, :], ACT.Sin, scale=TWO_PI / 2).then_inc(pgl_act, 1)

                with act.Fori(0, G8) as g:
                    it = l * G8 + g
                    n0, h0 = n_l + N_GATE + g * CH_PAIR, h_l + H_GATE + g * 2

                    def tables(j):
                        act.wait_ge(nf_ready, it * 4 + (j + 1))
                        act.wait_ge(tab_used, it * 4 + (j + 1))
                        own.do(A(tau[:, :], nf[:, :], ACT.Abs))
                        own.do(A(tab[:, 1::2, :], nf[:, :].unsqueeze(1).to_broadcast([P, 2, T]), ACT.Sin, scale=TWO_PI))
                        own.do(A(tab[:, 2, :], nf[:, :], ACT.Sin, scale=-TWO_PI))
                        own.wait()
                        A(tab[:, 0, :], tau[:, :], ACT.Sin, bias=HALF_PI, scale=-TWO_PI).then_inc(tab_ready, 1)

                    def lru():
                        act.wait_ge(ri_ready, it + 1)
                        act.wait_ge(yl_ready, it + 1)
                        own.do(A(trti[:, 0, :], ps[:, B_B, 0:T], ACT.Tanh, bias=pg[:, C_HBA:C_HBA + 1], scale=0.5))
                        A(trti[:, 1, :], ps[:, B_B, T:], ACT.Tanh, bias=pg[:, C_HBX:C_HBX + 1],
                          scale=0.5).then_inc(lru_act, 1)
                        own.wait()
                        own.chain(A(tw[:, :], trti[:, 0, :], ACT.Tanh, bias=pg[:, C_SP2:C_SP2 + 1],
                                    scale=pg[:, C_SP2:C_SP2 + 1]))
                        A(sq[:, :], tw[:, :], ACT.Sqrt).then_inc(decays_ready, 1)

                    def mla_q():
                        act.wait_ge(q_ready, it + 1)
                        A(qn[:, :], ps[:, B_A, 0:T], ACT.Copy).then_inc(qn_ready, 1)
                        act.dma_start(mlaw[:, 0:2 * KVR], mlaw_d[it, :, CQ * T:]).then_inc(kvw_loaded, 16)

                    def mla_kv():
                        act.wait_ge(kv_ready, it + 1)
                        A(kv[:, :, :].rearrange("p a t -> p (a t)"), ps[:, B_A, :], ACT.Copy).then_inc(kv_copied, 1)
                        act.dma_start(mlaw[:, :], mlaw_d[it + 1, :, 0:CQ * T]).then_inc(qw_loaded, 16)

                    def mla_exp():
                        act.wait_ge(max_ready, it + 1)
                        own.do(A(prob[:, 0, :], prob[:, 0, :], ACT.Exp, bias=row[:, 2:3], scale=SCALE,
                                 accum_out=row[:, 4:5]))
                        A(prob[:, 1:3, :], prob[:, 1:3, :], ACT.Exp, bias=row[:, 3:4], scale=SCALE,
                          accum_out=row[:, 5:6]).then_inc(prob_ready, 1)

                    def mla_turn():
                        act.wait_ge(pt_ready, it + 1)
                        A(probt[:, :, :].rearrange("p a t -> p (a t)"), ps[:, B_A, 0:3 * P], ACT.Copy).then_inc(pt_copied, 1)

                    def mla_out():
                        act.wait_ge(o_ready, it + 1)
                        act.wait_ge(iter_done, it + 1)
                        A(ym[:, :], ps[:, B_A, 0:T], ACT.Copy).then_inc(ym_ready, 1)

                    def gla_gate():
                        act.wait_ge(la_ready, it + 1)
                        A(ga[:, :], ps[:, B_B, 0:T], ACT.Abs, bias=pg[:, C_GLAB:C_GLAB + 1]).then_inc(la_abs, 1)
                        act.wait_ge(la_abs, it + 1)
                        own.chain(A(gb[:, :], ga[:, :], ACT.Exp, scale=-1.0))
                        A(gb[:, :], gb[:, :], ACT.Ln, bias=ONE).then_inc(la_act, 1)

                    def gla_decays():
                        act.wait_ge(cum_ready, it + 1)
                        own.do(A(ep[:, :], cum[:, :], ACT.Exp, scale=1.0 / TAU))
                        own.do(A(ga[:, :], cum[:, :], ACT.Exp, scale=-1.0 / TAU))
                        for c in range(4):
                            r = slice(64 * c, 64 * c + 64)
                            last = A(gb[:, r], cum[:, r], ACT.Exp, bias=tot[:, c:c + 1], scale=-1.0 / TAU)
                            if c < 3:
                                own.do(last)
                        last.then_inc(gla_exp, 1)

                    def gla_turn():
                        act.wait_ge(att_ready, it + 1)
                        A(probt[:, 0:2, :].rearrange("p a t -> p (a t)"), ps[:, B_A, T:], ACT.Copy).then_inc(ket_copied, 1)

                    def gla_out():
                        act.wait_ge(og_ready, it + 1)
                        act.wait_ge(iter_done, it + 1)
                        A(yg[:, :], ps[:, B_A, 0:T], ACT.Copy).then_inc(yg_ready, 1)

                    def next_mix():
                        act.wait_ge(bu_ready, it * 4 + 4)
                        act.wait_ge(cprime_ready, it + 1)
                        act.dma_start(mixw[:, :, :], mixw_d[it + 1]).then_inc(mix_loaded, 16)
                        act.dma_start(wg2[64:80, :], wg2_d[it + 1]).then_inc(wg2_loaded, 16)

                    act.wait_ge(iter_done, it + 1)
                    act.wait_ge(pg_ready, it + 1)
                    steps = {0: [lambda: tables(0)], 1: [mla_q], 3: [lru], 6: [mla_kv], 7: [lambda: tables(1), gla_gate],
                             9: [mla_exp], 13: [mla_turn], 14: [mla_out], 15: [lambda: tables(2)],
                             17: [gla_decays], 23: [lambda: tables(3)], 25: [gla_turn], 27: [next_mix], 30: [gla_out]}
                    for c in range(CH_PAIR):
                        if c == 0:
                            A(us[:, :], zb[:, g + Z_S5, :], ACT.Copy).then_inc(us_ready, 1)
                        hi(n0, c)
                        for step in steps.get(c, ()):
                            step()
                        if c == CH_HALF - 1:
                            evac(h0, 0, n0 + (c + 1))
                            act.wait_ge(acc_read, h0 + 3)
                            A(gate[:, 0, :, :], gate[:, 0, :, :], ACT.Silu).then_inc(silu_ready, 1)
                        if c == CH_PAIR - 1:
                            evac(h0 + 1, 1, n0 + (c + 1))
                            act.wait_ge(acc_read, h0 + 4)
                            own.do(A(gs5[:, g, :], gate[:, 1, 1, :], ACT.Silu))
                            A(gate[:, 1, 0, :], gate[:, 1, 0, :], ACT.Silu).then_inc(silu_ready, 1)
                    own.restart()

                act.wait_ge(iter_done, l * G8 + (G8 + 1))
                act.wait_ge(chunk_done, n_l + (N_GLU + W2))
                for q in range(4):
                    z = zb[:, Z_S5 + 2 * q:Z_S5 + 2 * q + 2, :]
                    own.chain(A(z, z, ACT.Gelu_apprx_tanh))
                    A(hb[:, 24 + 2 * q:26 + 2 * q, 0, :], z, ACT.Copy).then_inc(gelu_done, 1)
                act.wait_ge(cols_ready, c_l + 3)
                A(ncol[:, 0:4], ps[:, B_Y, 0:4], ACT.Sqrt, bias=EPS1, scale=1.0 / BR)
                A(ncol[:, 4:12], ps[:, B_Y, 4:12], ACT.Sqrt, bias=EPS1, scale=1.0 / (BR // 4)).then_inc(rms_ready, 1)
                for c in range(4 * CH_GLU):
                    hi(n_l + N_GLU, c)
                    if c >= 4:
                        split_hi(c - 4, l * 32 + (16 + c - 4 + 1))
                    if c % CH_GLU == CH_GLU - 1:
                        m = c // CH_GLU
                        evac(h_l + (H_GLU + m), m % 2, n_l + (N_GLU + c + 1))
                        act.wait_ge(acc_read, h_l + (H_GLU + m + 3))
                        own.do(A(gate[:, m % 2, 0, :], gate[:, m % 2, 0, :], ACT.Tanh,
                                 bias=lru8[:, 5, 2 * m:2 * m + 1], scale=0.5))
                        A(gate[:, m % 2, 1, :], gate[:, m % 2, 1, :], ACT.Tanh,
                          bias=lru8[:, 5, 2 * m + 1:2 * m + 2], scale=0.5).then_inc(glu_tanh, 1)
                for h in range(2):
                    if h == 0:
                        act.wait_ge(x_stored, 16 * (16 * l + 1))
                    act.wait_ge(y2_ready, 4 * l + 4)
                    act.dma_start(gate[:, h, :, :], xres[:, 2 * h:2 * h + 2, :]).then_inc(xold_loaded[h], 16)

                def out_end(i, h, more):
                    evac(h_l + H_OUT + (i * 2 + h), h, n_l + N_OUT + (i * CH_PAIR + CH_HALF * (h + 1)))
                    act.wait_ge(outx, l * 16 + (i * 2 + (h + 1)))
                    act.dma_start(xres[:, bass.ds(i * 4 + 2 * h, 2), :], zb[:, bass.ds(i * 4 + 2 * h, 2), :]).then_inc(x_stored, 16)
                    if more:
                        act.dma_start(gate[:, h, :, :], xres[:, bass.ds(i * 4 + (4 + 2 * h), 2), :]).then_inc(xold_loaded[h], 16)

                for c in range(CH_PAIR):
                    if c == 6:
                        rms(c_l + 4, 2, BR, EPS4)
                    hi(n_l + N_OUT, c)
                    if 9 <= c < 13:
                        split_hi(c + 3, l * 32 + (16 + c + 3 + 1))
                    if c % CH_HALF == CH_HALF - 1:
                        out_end(0, c // CH_HALF, True)
                own.restart()
                with act.Fori(1, 7) as i:
                    for c in range(CH_PAIR):
                        hi(n_l + N_OUT + i * CH_PAIR, c)
                        if c % CH_HALF == CH_HALF - 1:
                            out_end(i, c // CH_HALF, True)
                for c in range(CH_PAIR):
                    hi(n_l + (N_OUT + 7 * CH_PAIR), c)
                    if c % CH_HALF == CH_HALF - 1:
                        out_end(7, c // CH_HALF, False)
            rms(4 * L + 1, 2, D, EPS1)

        @block.vector
        def _(dve):
            own = Own(dve, dve_own)
            V = nc.vector

            def lo(n0, c):
                s, d = (c + LOOK) % RAW, (c + LOOK) % W2
                dve.wait_ge(hi_ready, n0 + (c + LOOK + 1))
                V.tensor_tensor(w2[:, d, :, 1, :], raw[:, s, :, :], w2[:, d, :, 0, :].bitcast(F),
                                ALU.subtract).then_inc(w2_ready, 1)

            def evac(h0, half, dst, tiles=2):
                dve.wait_ge(lo_copied, h0 + 1)
                V.tensor_tensor(dst, half_lo[:, 0:tiles, :], ps[:, 2 * half:2 * half + tiles, T:],
                                ALU.add).then_inc(acc_read, 1)

            def reciprocals(count, cols):
                dve.wait_ge(rms_ready, count)
                V.reciprocal(rcol[:, 0:cols], ncol[:, 0:cols]).then_inc(rcol_ready, 1)

            def h_mul(c, n):
                if c >= 2:
                    dve.wait_ge(h_ready, n + (c - 1))
                for q in range(2):
                    k = 2 * c + q
                    last = V.scalar_tensor_tensor(out=hf[c % 2][:, q, :], in0=zb[:, k, :], scalar=sm[:, k:k + 1],
                                                  in1=ps[:, B_BU, 0:T], op0=ALU.mult, op1=ALU.mult)
                last.then_inc(hf_ready, 1)

            def y_mul(k, n):
                if k >= 2:
                    dve.wait_ge(h_ready, n + (k - 1))
                if k < 4:
                    src, r = zb[:, 2 * k:2 * k + 2, :], ps[:, B_BU, 0:T]
                elif k < 8:
                    q = k - 4
                    src = vb[:, 2 * q:2 * q + 2, :, :].rearrange("p g t d -> p g (t d)")
                    r = ps[:, B_A + q // 2, T * (q % 2):T * (q % 2) + T]
                elif k < 12:
                    src, r = ymla[:, 2 * k - 16:2 * k - 14, :], ps[:, B_BU, T:]
                else:
                    src, r = gs5[:, 2 * k - 24:2 * k - 22, :], ps[:, B_Y, 0:T]
                V.tensor_tensor(hf[k % 2][:, :, :], src, r.unsqueeze(1).to_broadcast([P, 2, T]),
                                ALU.mult).then_inc(hf_ready, 1)

            def split_lo(k, count):
                dve.wait_ge(h_hi_ready, count)
                V.tensor_tensor(hb[:, 2 * k:2 * k + 2, 1, :], hf[k % 2][:, :, :],
                                hb[:, 2 * k:2 * k + 2, 0, :].bitcast(F), ALU.subtract).then_inc(h_ready, 1)

            dve.sem_inc(acc_read, 2)
            dve.sem_inc(iter_done, 1)
            dve.sem_inc(st_ready, 1)
            dve.sem_inc(tab_used, 1)
            dve.sem_inc(bu_read, 1)
            dve.sem_inc(yl_ready, 1)
            for i in range(8):
                dve.wait_ge(squares_made, i + 1)
                V.tensor_reduce(sx[:, :] if i == 0 else tau[:, :],
                                gs5[:, 4 * (i % 2):4 * (i % 2) + 4, :].rearrange("p a t -> p t a"), AX.X,
                                ALU.add).then_inc(x_ready, 1)
                if i:
                    dve.wait_ge(x_ready, i + 1)
                    own.chain(V.tensor_tensor(sx[:, :], sx[:, :], tau[:, :], ALU.add))
            dve.sem_inc(sx_first, 1)
            for s in range(LOOK):
                dve.wait_ge(hi_ready, s + 1)
                V.tensor_tensor(w2[:, s, :, 1, :], raw[:, s, :, :], w2[:, s, :, 0, :].bitcast(F),
                                ALU.subtract).then_inc(w2_ready, 1)
            C1 = 6.28125
            C2 = float(np.floor((2 * np.pi - C1) * 2.0 ** 21) / 2.0 ** 21)
            C3 = float(2 * np.pi - C1 - C2)
            dve.wait_ge(const_loaded, 16)
            dve.wait_ge(pos_loaded, 16)
            own.chain(V.tensor_copy(ga[:, :], posi[:, :]))
            own.chain(V.tensor_scalar(ga[:, :], ga[:, :], kc[:, K_INVF:K_INVF + 1], None, ALU.mult))
            own.chain(V.tensor_scalar(gb[:, :], ga[:, :], 1.0 / (2 * np.pi), MAGIC, ALU.mult, ALU.add))
            own.chain(V.tensor_scalar(gb[:, :], gb[:, :], -MAGIC, None, ALU.add))
            for part in (C1, C2, C3):
                own.chain(V.scalar_tensor_tensor(out=ga[:, :], in0=gb[:, :], scalar=-part, in1=ga[:, :],
                                                 op0=ALU.mult, op1=ALU.add))
            V.tensor_scalar(ga[:, :], ga[:, :], 3.1415925, -3.1415925, ALU.min, ALU.max).then_inc(rope_made, 1)
            dve.wait_ge(rope_made, 1)
            dve.wait_ge(small_loaded, 48)
            dve.wait_ge(consts_made, 1)
            own.restart()

            with dve.Fori(0, L) as l:
                n_l, h_l, c_l = l * N_LAYER, l * H_LAYER, l * 4

                def lru_abs():
                    lam = pgl[:, :, C_LAM]
                    own.do(V.tensor_copy(pgl[:, :, 0:NPG_IN], pg_all[:, l, :, :]))
                    own.do(V.tensor_copy(s5[:, 0:3, :], s5_all[:, l, :, :]))
                    own.chain(V.tensor_scalar(lru8[:, 5, :], sm[:, S_BGLU:S_BGLU + G8], 0.5, None, ALU.mult))
                    own.do(V.tensor_scalar(pgl[:, :, C_HBA:C_HBX + 1], pgl[:, :, C_BA:C_BX + 1], 0.5, None, ALU.mult))
                    own.do(V.tensor_scalar(lru8[:, 3, :], lam, -1.0, 0.0, ALU.mult, ALU.max))
                    own.chain(V.tensor_scalar(lru8[:, 2, :], lam, -1.0, None, ALU.mult))
                    V.tensor_tensor(lru8[:, 0, :], lru8[:, 2, :], lam, ALU.max).then_inc(pgl_dve, 1)

                def lru_softplus():
                    dve.wait_ge(pgl_act, 2 * l + 1)
                    e, z, z2, a = lru8[:, 1, :], lru8[:, 0, :], lru8[:, 2, :], lru8[:, 4, :]
                    own.chain(V.tensor_scalar(z, e, 2.0, None, ALU.add))
                    own.chain(V.reciprocal(z, z))
                    own.chain(V.tensor_tensor(z, z, e, ALU.mult))
                    own.chain(V.tensor_tensor(z2, z, z, ALU.mult))
                    own.chain(V.tensor_scalar(a, z2, 1.0 / 17, None, ALU.mult))
                    for k in range(15, 1, -2):
                        own.chain(V.scalar_tensor_tensor(out=a, in0=a, scalar=1.0 / k, in1=z2, op0=ALU.add, op1=ALU.mult))
                    own.chain(V.scalar_tensor_tensor(out=a, in0=a, scalar=1.0, in1=z, op0=ALU.add, op1=ALU.mult))
                    own.chain(V.scalar_tensor_tensor(out=a, in0=a, scalar=2.0, in1=lru8[:, 3, :], op0=ALU.mult,
                                                     op1=ALU.add))
                    V.tensor_scalar(pgl[:, :, C_SP2], a, 2.0, None, ALU.mult).then_inc(pgl_dve, 1)

                def rows(a, n=1):
                    return s5[:, a:a + n, :]

                def expm1_small(dst, src, tmp, n):
                    t, p, m = rows(src, n), rows(dst, n), rows(tmp, n)
                    own.chain(V.tensor_scalar(t, t, 1.0 / 1024, None, ALU.mult))
                    own.chain(V.tensor_scalar(p, t, 1.0 / 5, 1.0, ALU.mult, ALU.add))
                    for k in (4, 3, 2):
                        own.chain(V.tensor_tensor(m, p, t, ALU.mult))
                        own.chain(V.tensor_scalar(p, m, 1.0 / k, 1.0, ALU.mult, ALU.add))
                    own.chain(V.tensor_tensor(p, p, t, ALU.mult))

                def square_up(dst, n, times):
                    p = rows(dst, n)
                    for _ in range(times):
                        own.chain(V.scalar_tensor_tensor(out=p, in0=p, scalar=2.0, in1=p, op0=ALU.add, op1=ALU.mult))

                def s5_relu():
                    own.do(V.tensor_scalar(rows(3), rows(0), 0.0, None, ALU.max))
                    own.chain(V.tensor_scalar(rows(4), rows(0), -1.0, 0.0, ALU.mult, ALU.max))
                    expm1_small(10, 3, 12, 2)

                def s5_dt():
                    own.chain(V.tensor_scalar(rows(10, 2), rows(10, 2), 1.0, None, ALU.add))
                    own.chain(V.reciprocal(rows(11), rows(11)))
                    own.chain(V.tensor_tensor(rows(3), rows(10), rows(11), ALU.mult))
                    own.chain(V.tensor_tensor(rows(4), rows(1), rows(3), ALU.mult))

                def s5_turns():
                    own.chain(V.tensor_tensor(rows(6), rows(2), rows(3), ALU.mult))
                    own.chain(V.tensor_scalar(rows(6), rows(6), 1.0 / (2 * np.pi), None, ALU.mult))
                    own.chain(V.tensor_scalar(rows(7), rows(6), MAGIC, None, ALU.add))
                    own.chain(V.tensor_scalar(rows(7), rows(7), -MAGIC, None, ALU.add))
                    V.tensor_tensor(rows(7), rows(6), rows(7), ALU.subtract).then_inc(pgl_dve, 1)

                def pcol(c):
                    return pgl[:, :, c:c + 4]

                def s5_scale():
                    dve.wait_ge(pgl_act, 2 * l + 2)
                    own.do(V.tensor_scalar(rows(10), rows(5), 1.0, None, ALU.add))
                    own.chain(V.tensor_tensor(rows(11), rows(9), rows(9), ALU.mult))
                    own.chain(V.scalar_tensor_tensor(out=rows(11), in0=rows(11), scalar=-2.0, in1=rows(10),
                                                     op0=ALU.mult, op1=ALU.mult))
                    own.chain(V.tensor_tensor(rows(11), rows(11), rows(5), ALU.add))
                    own.chain(V.tensor_tensor(rows(12), rows(10), rows(8), ALU.mult))
                    own.chain(V.tensor_tensor(rows(13), rows(1), rows(1), ALU.mult))
                    own.chain(V.tensor_tensor(rows(14), rows(2), rows(2), ALU.mult))
                    own.chain(V.tensor_tensor(rows(13), rows(13), rows(14), ALU.add))
                    own.chain(V.reciprocal(rows(13), rows(13)))

                def s5_scale2():
                    own.do(V.tensor_tensor(rows(14), rows(11), rows(1), ALU.mult))
                    own.do(V.tensor_tensor(rows(15), rows(12), rows(2), ALU.mult))
                    own.do(V.tensor_tensor(rows(16), rows(11), rows(2), ALU.mult))
                    own.chain(V.tensor_tensor(rows(17), rows(12), rows(1), ALU.mult))
                    own.do(V.tensor_tensor(rows(14), rows(14), rows(15), ALU.add))
                    own.chain(V.tensor_tensor(rows(16), rows(16), rows(17), ALU.subtract))
                    view = lambda a: s5[:, a, :].rearrange("p (g j) -> p g j", j=4)
                    own.do(V.tensor_tensor(pcol(C_SR), view(14), view(13), ALU.mult))
                    own.do(V.tensor_tensor(pcol(C_NSI), view(16), view(13), ALU.mult))
                    own.do(V.tensor_copy(pcol(C_R), view(10)))
                    V.tensor_copy(pcol(C_F0), view(7)).then_inc(dve_prep, 1)

                def k_rotate():
                    dve.wait_ge(act_prep, 4)
                    dve.wait_ge(kperm_ready, l + 1)
                    V.tensor_tensor(qr[:, :], ps[:, B_A, 0:T], rope[:, :], ALU.mult).then_inc(krot_ready, 1)

                def k_keep():
                    dve.wait_ge(ksum_ready, l + 1)
                    V.tensor_copy(kext[:, :], ps[:, B_A, 0:T]).then_inc(kext_ready, 1)

                def latent(k):
                    if k == 0:
                        dve.wait_ge(rstd_ready, c_l + 2)
                    r = ps[:, B_B, 0:T] if k < CQ else ps[:, B_B, T:]
                    V.scalar_tensor_tensor(out=zb[:, Z_CQ + k, :], in0=zb[:, Z_CQ + k, :],
                                           scalar=sm[:, S_QG + k:S_QG + k + 1], in1=r, op0=ALU.mult,
                                           op1=ALU.mult).then_inc(latents_ready, 1)

                own.chain(V.tensor_copy(sm[:, :], sm_all[:, l, :]))
                reciprocals(c_l + 1, 2)
                dve.wait_ge(rstd_ready, c_l + 1)
                h_mul(0, l * 32)
                for c in range(CH_PAIR):
                    if c < CH_HALF - 1:
                        h_mul(c + 1, l * 32)
                    if c < CH_HALF:
                        split_lo(c, l * 32 + (c + 1))
                    lo(n_l, c)
                    if c == CH_HALF - 1:
                        dve.wait_ge(x_stored, 16 * (16 * l + 1))
                    if c % CH_HALF == CH_HALF - 1:
                        h = c // CH_HALF
                        evac(h_l + h, h, zb[:, 2 * h:2 * h + 2, :])
                own.restart()
                with dve.Fori(1, 8) as i:
                    for c in range(CH_PAIR):
                        lo(n_l + i * CH_PAIR, c)
                        if c % CH_HALF == CH_HALF - 1:
                            h = c // CH_HALF
                            evac(h_l + (i * 2 + h), h, zb[:, bass.ds(i * 4 + 2 * h, 2), :])
                for c in range(CH_PAIR):
                    lo(n_l + 8 * CH_PAIR, c)
                    if c == CH_HALF - 1:
                        evac(h_l + 16, 0, zb[:, KT:KT + 2, :])
                    if c == CH_PAIR - 1:
                        evac(h_l + 17, 1, kg[:, :].unsqueeze(1), 1)
                steps = {4: [k_rotate], 7: [k_keep], 9: [lru_abs], 11: [lru_softplus], 13: [s5_relu],
                         16: [lambda: square_up(10, 2, 5)], 18: [lambda: square_up(10, 2, 5)], 20: [s5_dt],
                         22: [lambda: reciprocals(c_l + 2, 4)], 24: [lambda: expm1_small(5, 4, 12, 1)],
                         26: [lambda: square_up(5, 1, 5)], 28: [lambda: square_up(5, 1, 5)], 30: [s5_turns],
                         36: [s5_scale], 38: [s5_scale2]}
                for k in range(CQ + CKV):
                    steps[40 + 2 * k] = [lambda k=k: latent(k)]
                for c in range(2 * CH_PAIR):
                    lo(n_l + N_V, c)
                    for step in steps.get(c, ()):
                        step()
                    if c % CH_HALF == CH_HALF - 1:
                        h = c // CH_HALF
                        evac(h_l + (H_V + h), h % 2, vb[:, 2 * h:2 * h + 2, :, :].rearrange("p g t d -> p t g d"))
                own.restart()

                with dve.Fori(0, G8) as g:
                    it = l * G8 + g
                    n0, h0 = n_l + N_GATE + g * CH_PAIR, h_l + H_GATE + g * 2

                    def s5_rotate(j):
                        dve.wait_ge(bu_ready, it * 4 + (j + 1))
                        dve.wait_ge(tab_ready, it * 4 + (j + 2))
                        dve.wait_ge(state_used, it * 4 + (j + 1))
                        bu = ps[:, B_BU, :].rearrange("p (a t) -> p a t", a=2)
                        own.do(V.tensor_tensor(xx[:, :, :], bu, tab[:, 0:1, :].to_broadcast([P, 2, T]), ALU.mult))
                        V.tensor_tensor(yy[:, :, :], bu[:, ::-1, :], tab[:, 2:4, :], ALU.mult).then_inc(bu_read, 1)

                    def s5_sum(j):
                        own.wait()
                        dve.wait_ge(bu_read, it * 4 + (j + 2))
                        own.do(V.tensor_tensor(xx[:, :, :], xx[:, :, :], yy[:, :, :], ALU.add))

                    def s5_scan(j):
                        own.wait()
                        for a in range(2):
                            own.do(V.tensor_tensor_scan(g2[:, a, :], pg[:, C_R + j:C_R + j + 1].to_broadcast([P, T]),
                                                        xx[:, a, :], 0.0, ALU.mult, ALU.add))

                    def s5_back(j):
                        own.wait()
                        own.do(V.tensor_tensor(xx[:, :, :], g2[:, :, :], tab[:, 0:1, :].to_broadcast([P, 2, T]), ALU.mult))

                    def s5_back2(j):
                        own.wait()
                        V.tensor_tensor(yy[:, :, :], g2[:, ::-1, :], tab[:, 1:3, :], ALU.mult).then_inc(tab_used, 1)

                    def s5_state(j):
                        dve.wait_ge(tab_used, it * 4 + (j + 2))
                        V.tensor_tensor(xx[:, :, :], xx[:, :, :], yy[:, :, :], ALU.add).then_inc(state_ready, 1)

                    def conv():
                        own.chain(V.tensor_scalar(xc[:, :], zb[:, g, :], pg[:, C_CONV + 3:C_CONV + 4],
                                                  pg[:, C_CONVB:C_CONVB + 1], ALU.mult, ALU.add))
                        for d in (1, 2, 3):
                            last = V.scalar_tensor_tensor(out=xc[:, d:], in0=zb[:, g, 0:T - d],
                                                          scalar=pg[:, C_CONV + 3 - d:C_CONV + 4 - d], in1=xc[:, d:],
                                                          op0=ALU.mult, op1=ALU.add)
                            if d < 3:
                                own.chain(last)
                        last.then_inc(xc_ready, 1)

                    def lru_den():
                        dve.wait_ge(decays_ready, it + 1)
                        own.chain(V.tensor_scalar(ke[:, :], tw[:, :], 1.0, None, ALU.add))
                        own.chain(V.reciprocal(ki[:, :], ke[:, :]))

                    def lru_in():
                        own.do(V.scalar_tensor_tensor(out=ke[:, :], in0=trti[:, 1, :], scalar=1.0, in1=xc[:, :],
                                                      op0=ALU.add, op1=ALU.mult))
                        own.do(V.tensor_scalar(tw[:, :], ki[:, :], 2.0, -1.0, ALU.mult, ALU.add))
                        own.chain(V.tensor_tensor(sq[:, :], sq[:, :], ki[:, :], ALU.mult))
                        own.chain(V.tensor_tensor(ke[:, :], ke[:, :], sq[:, :], ALU.mult))

                    def lru_scan():
                        V.tensor_tensor_scan(yl[:, :], tw[:, :], ke[:, :], 0.0, ALU.mult, ALU.add).then_inc(yl_ready, 1)

                    def q_rotate():
                        dve.wait_ge(qn_ready, it + 1)
                        V.tensor_tensor(qr[:, :], ps[:, B_A, T:], rope[:, :], ALU.mult).then_inc(qr_ready, 1)

                    def row_max():
                        dve.wait_ge(sc_ready, it + 1)
                        own.pause()
                        own.do(V.tensor_tensor_reduce(prob[:, 0, :], ps[:, B_A, 0:P], kc[:, K_AMASK + P:K_AMASK + 2 * P], 1.0,
                                                      -3.0e38, ALU.add, ALU.max, row[:, 0:1]))
                        own.do(V.tensor_tensor_reduce(prob[:, 1:3, :].rearrange("p a t -> p (a t)"), ps[:, B_A, P:3 * P],
                                                      kc[:, K_AMASK:K_AMASK + 2 * P], 1.0, -3.0e38, ALU.add, ALU.max,
                                                      row[:, 1:2]))
                        own.wait()
                        V.tensor_scalar(row[:, 2:4], row[:, 0:2], -SCALE, None, ALU.mult).then_inc(max_ready, 1)

                    def prob_norm():
                        dve.wait_ge(prob_ready, it + 1)
                        own.chain(V.reciprocal(row[:, 6:8], row[:, 4:6]))
                        own.do(V.tensor_scalar(prob[:, 0, :], prob[:, 0, :], row[:, 6:7], None, ALU.mult))
                        own.wait()
                        V.tensor_scalar(prob[:, 1:3, :], prob[:, 1:3, :], row[:, 7:8], None,
                                        ALU.mult).then_inc(probn_ready, 1)

                    def gla_log():
                        dve.wait_ge(la_act, it + 1)
                        own.chain(V.tensor_scalar(qd[:, :], ps[:, B_B, 0:T], pg[:, C_GLAB:C_GLAB + 1], 0.0, ALU.add, ALU.min))
                        own.chain(V.tensor_tensor(qd[:, :], qd[:, :], gb[:, :], ALU.subtract))
                        own.chain(V.tensor_tensor_scan(cum[:, :], kc[:, K_CMASK:K_CMASK + T], qd[:, :], 0.0, ALU.mult,
                                                       ALU.add))
                        V.tensor_scalar(tot[:, :], cum[:, 63::64], 1.0 / TAU, None, ALU.mult).then_inc(cum_ready, 1)

                    def gla_qk():
                        dve.wait_ge(gla_exp, it + 1)
                        q, k = zb[:, g // 2 + Z_Q, :], zb[:, g // 2 + Z_K, :]
                        own.do(V.scalar_tensor_tensor(out=qd[:, :], in0=q, scalar=float(P) ** -0.5, in1=ep[:, :],
                                                      op0=ALU.mult, op1=ALU.mult))
                        own.do(V.tensor_tensor(ki[:, :], k, ga[:, :], ALU.mult))
                        own.wait()
                        V.tensor_tensor(ke[:, :], k, gb[:, :], ALU.mult).then_inc(qk_ready, 1)

                    def gla_mask():
                        dve.wait_ge(ket_copied, it + 1)
                        own.pause()
                        m = kc[:, K_GMASK:K_GMASK + P].bitcast(I).unsqueeze(1).to_broadcast([P, 2, P])
                        V.copy_predicated(attm[:, :, :], m, ps[:, B_A, 0:T].rearrange("p (b s) -> p b s", b=2))\
                            .then_inc(att_masked, 1)

                    def gla_state():
                        dve.wait_ge(kvs_ready, it * 2 + 2)
                        own.chain(V.tensor_copy(st[:, 0, :], ps[:, B_B, 0:P]))
                        for c in (1, 2):
                            last = V.scalar_tensor_tensor(out=st[:, c, :], in0=st[:, c - 1, :],
                                                          scalar=ep[:, 64 * c + 63:64 * c + 64],
                                                          in1=ps[:, B_B, P * c:P * c + P], op0=ALU.mult, op1=ALU.add)
                            if c == 1:
                                own.chain(last)
                        last.then_inc(st_ready, 1)

                    dve.wait_ge(pg_ready, it + 1)
                    steps = {0: [conv], 2: [q_rotate], 7: [lru_den], 8: [row_max, lru_in], 10: [lru_scan],
                             11: [prob_norm], 15: [gla_log], 23: [gla_qk], 26: [gla_mask], 27: [gla_state]}
                    for j in range(4):
                        for d, f in ((1, s5_rotate), (2, s5_sum), (3, s5_scan), (4, s5_back), (5, s5_back2), (6, s5_state)):
                            steps.setdefault(8 * j + d, []).insert(0, lambda f=f, j=j: f(j))
                    for c in range(CH_PAIR):
                        lo(n0, c)
                        for step in steps.get(c, ()):
                            step()
                        if c % CH_HALF == CH_HALF - 1:
                            h = c // CH_HALF
                            evac(h0 + h, h, gate[:, h, :, :])
                    dve.wait_ge(silu_ready, it * 2 + 2)
                    dve.wait_ge(yl_squared, it + 1)
                    dve.wait_ge(ym_squared, it + 1)
                    dve.wait_ge(yg_ready, it + 2)
                    for dst, y, c_gain, gt in ((zb[:, g, :], yl, C_LRUG, gate[:, 0, 0, :]),
                                               (ymla[:, g, :], ym, C_MLAG, gate[:, 0, 1, :]),
                                               (vb[:, g, :, :].rearrange("p t d -> p (t d)"), yg, C_GLAG, gate[:, 1, 0, :])):
                        own.do(V.scalar_tensor_tensor(out=dst, in0=y[:, :], scalar=pg[:, c_gain:c_gain + 1], in1=gt,
                                                      op0=ALU.mult, op1=ALU.mult))
                    dve.wait_ge(state_used, it * 4 + 5)
                    own.chain(V.scalar_tensor_tensor(out=zb[:, g + Z_S5, :], in0=us[:, :], scalar=pg[:, C_S5D:C_S5D + 1],
                                                     in1=ps[:, B_Y, 0:T], op0=ALU.mult, op1=ALU.add))
                    dve.wait_ge(yg_squared, it + 1)
                    dve.sem_inc(iter_done, 1)
                    own.restart()

                for q in range(4):
                    dve.wait_ge(gelu_done, l * 4 + (q + 1))
                    V.tensor_tensor(hb[:, 24 + 2 * q:26 + 2 * q, 1, :], zb[:, Z_S5 + 2 * q:Z_S5 + 2 * q + 2, :],
                                    hb[:, 24 + 2 * q:26 + 2 * q, 0, :].bitcast(F), ALU.subtract).then_inc(glu_ready, 1)
                reciprocals(c_l + 3, 12)
                for c in range(4 * CH_GLU):
                    lo(n_l + N_GLU, c)
                    if c == 3:
                        dve.wait_ge(rstd_ready, c_l + 3)
                    if 3 <= c < 15:
                        y_mul(c - 3, l * 32 + 16)
                    if c >= 4:
                        split_lo(c - 4, l * 32 + (16 + c - 4 + 1))
                    if c % CH_GLU == CH_GLU - 1:
                        m = c // CH_GLU
                        evac(h_l + (H_GLU + m), m % 2, gate[:, m % 2, :, :])
                        z = zb[:, Z_S5 + 2 * m:Z_S5 + 2 * m + 2, :]
                        dve.wait_ge(glu_tanh, l * 4 + (m + 1))
                        V.scalar_tensor_tensor(out=z, in0=gate[:, m % 2, :, :], scalar=1.0, in1=z, op0=ALU.add,
                                               op1=ALU.mult).then_inc(y2_ready, 1)
                        dve.wait_ge(y2_ready, l * 4 + (m + 1))
                        for q in range(2):
                            k = 2 * m + q
                            own.do(V.scalar_tensor_tensor(out=gs5[:, k, :], in0=zb[:, Z_S5 + k, :],
                                                          scalar=sm[:, S_S5G + k:S_S5G + k + 1], in1=gs5[:, k, :],
                                                          op0=ALU.mult, op1=ALU.mult))
                own.wait()

                def out_end(i, h):
                    z = zb[:, bass.ds(i * 4 + 2 * h, 2), :]
                    evac(h_l + H_OUT + (i * 2 + h), h, z)
                    dve.wait_ge(acc_read, h_l + H_OUT + (i * 2 + (h + 3)))
                    dve.wait_ge(xold_loaded[h], l * 128 + (i * 16 + 16))
                    V.tensor_tensor(z, z, gate[:, h, :, :], ALU.add).then_inc(outx, 1)

                for c in range(CH_PAIR):
                    if c == 6:
                        reciprocals(c_l + 4, 2)
                    lo(n_l + N_OUT, c)
                    if c == 9:
                        dve.wait_ge(rstd_ready, c_l + 4)
                    if 9 <= c < 13:
                        y_mul(c + 3, l * 32 + 16)
                    if 10 <= c < 14:
                        split_lo(c + 2, l * 32 + (16 + c + 2 + 1))
                    if c == CH_HALF - 1:
                        dve.wait_ge(glu_squared, l * 4 + 4)
                    if c % CH_HALF == CH_HALF - 1:
                        out_end(0, c // CH_HALF)
                own.restart()
                with dve.Fori(1, 8) as i:
                    for c in range(CH_PAIR):
                        lo(n_l + N_OUT + i * CH_PAIR, c)
                        if c % CH_HALF == CH_HALF - 1:
                            out_end(i, c // CH_HALF)

            reciprocals(4 * L + 1, 2)
            dve.wait_ge(rstd_ready, 4 * L + 1)
            dve.wait_ge(x_stored, 16 * (16 * L + 1))
            for k in range(KT):
                last = V.scalar_tensor_tensor(out=zb[:, k, :], in0=zb[:, k, :], scalar=sm[:, S_FG + k:S_FG + k + 1],
                                              in1=ps[:, B_BU, 0:T], op0=ALU.mult, op1=ALU.mult)
                if k % 8 == 7:
                    last.then_inc(outx_ready, 1)

        @block.gpsimd
        def _(pool):
            own = Own(pool, pool_own)
            G = nc.gpsimd
            own.do(G.memset(ones[:, :], 1.0))
            own.do(G.memset(cst[:, 0:1], EPS))
            own.do(G.memset(cst[:, 1:2], 4 * EPS))
            own.do(G.memset(cst[:, 2:3], float(np.pi / 2)))
            own.do(G.memset(cst[:, 3:4], 1.0))
            own.do(G.memset(attm[:, :, :], 0.0))
            own.wait()
            pool.sem_inc(consts_made, 1)
            pool.wait_ge(sx_first, 1)
            pool.sem_inc(sx_ready, 1)
            pool.wait_ge(const_loaded, 16)
            own.restart()

            def add_square(dst, src, done):
                own.chain(G.tensor_tensor(sqp[:, :], src, src, ALU.mult))
                G.tensor_tensor(dst, dst, sqp[:, :], ALU.add).then_inc(done, 1)

            with pool.Fori(0, L) as l:
                h_l, c_l = l * H_LAYER, l * 4
                pool.wait_ge(acc_read, h_l + 16 + 3)
                for k in range(CQ + CKV):
                    dst, z = ssq[:, 2 if k < CQ else 3, :], zb[:, Z_CQ + k, :]
                    if k in (0, CQ):
                        G.tensor_tensor(dst, z, z, ALU.mult).then_inc(latent_squared, 1)
                    else:
                        add_square(dst, z, latent_squared)
                    pool.wait_ge(latent_squared, 10 * l + (k + 1))
                pool.wait_ge(cols_ready, c_l + 2)
                own.pause()
                own.chain(G.memset(ssq[:, :, :], 0.0))
                pool.wait_ge(dve_prep, l + 1)
                own.restart()
                with pool.Fori(0, G8) as g:
                    it = l * G8 + g
                    pool.wait_ge(iter_done, it + 1)
                    G.tensor_copy(pg[:, :], pgl[:, g, :]).then_inc(pg_ready, 1)
                    pool.wait_ge(pg_ready, it + 1)

                    def turns(j):
                        f0 = pg[:, C_F0 + j:C_F0 + j + 1]
                        iota = kc[:, K_IOTA:K_IOTA + T]
                        pool.wait_ge(tab_ready, it * 4 + (j + 1))
                        own.pause()
                        own.do(G.tensor_scalar(tau[:, :], iota, f0, None, ALU.mult))
                        own.chain(G.tensor_scalar(nf[:, :], iota, f0, MAGIC, ALU.mult, ALU.add))
                        own.chain(G.tensor_scalar(nf[:, :], nf[:, :], -MAGIC, None, ALU.add))
                        G.tensor_tensor(nf[:, :], nf[:, :], tau[:, :], ALU.subtract).then_inc(nf_ready, 1)
                        pool.wait_ge(nf_ready, it * 4 + (j + 1))

                    turns(0)
                    pool.wait_ge(mix_loaded, it * 16 + 16)
                    pool.wait_ge(state_used, it * 4 + 1)
                    cr = mixw[:, 4, :].rearrange("p (j h) -> p j h", j=4)
                    ci = mixw[:, 5, :].rearrange("p (j h) -> p j h", j=4)
                    sr = pg[:, C_SR:C_SR + 4].unsqueeze(2).to_broadcast([P, 4, 32])
                    nsi = pg[:, C_NSI:C_NSI + 4].unsqueeze(2).to_broadcast([P, 4, 32])
                    t0 = sqp[:, 0:P].rearrange("p (j h) -> p j h", j=4)
                    t1 = sqp[:, P:T].rearrange("p (j h) -> p j h", j=4)
                    own.do(G.tensor_tensor(t0, cr, sr, ALU.mult))
                    own.chain(G.tensor_tensor(t1, ci, nsi, ALU.mult))
                    own.chain(G.tensor_tensor(cprime[:, 0, :, :], t0, t1, ALU.add))
                    own.do(G.tensor_tensor(t0, cr, nsi, ALU.mult))
                    own.chain(G.tensor_tensor(t1, ci, sr, ALU.mult))
                    G.tensor_tensor(cprime[:, 1, :, :], t0, t1, ALU.subtract).then_inc(cprime_ready, 1)
                    pool.wait_ge(cprime_ready, it + 1)
                    own.do(G.tensor_copy(vs[:, :, :], vb[:, g, :, :]))
                    own.wait()
                    pool.sem_inc(vs_ready, 1)
                    turns(1)
                    turns(2)
                    pool.wait_ge(yl_ready, it + 2)
                    add_square(ssq[:, 0, :], yl[:, :], yl_squared)
                    pool.wait_ge(yl_squared, it + 1)
                    pool.wait_ge(ym_ready, it + 2)
                    add_square(ssq[:, 1, :], ym[:, :], ym_squared)
                    pool.wait_ge(ym_squared, it + 1)
                    turns(3)
                    pool.wait_ge(yg_ready, it + 2)
                    add_square(ssq[:, g // 2 + 2, :], yg[:, :], yg_squared)
                    pool.wait_ge(yg_squared, it + 1)
                    own.restart()
                for m in range(4):
                    pool.wait_ge(y2_ready, l * 4 + (m + 1))
                    for q in range(2):
                        z = zb[:, Z_S5 + 2 * m + q, :]
                        if m + q:
                            own.chain(G.tensor_tensor(sqp[:, :], z, z, ALU.mult))
                            last = G.tensor_tensor(sx[:, :], sx[:, :], sqp[:, :], ALU.add)
                        else:
                            last = G.tensor_tensor(sx[:, :], z, z, ALU.mult)
                        if q == 0:
                            own.chain(last)
                    last.then_inc(glu_squared, 1)
                    pool.wait_ge(glu_squared, l * 4 + (m + 1))
                pool.wait_ge(cols_ready, c_l + 4)
                own.pause()
                own.chain(G.memset(sx[:, :], 0.0))
                own.restart()
                with pool.Fori(0, 8) as i:
                    for h in range(2):
                        pool.wait_ge(outx, l * 16 + (i * 2 + (h + 1)))
                        for q in range(2):
                            z = zb[:, i * 4 + (2 * h + q), :]
                            own.chain(G.tensor_tensor(sqp[:, :], z, z, ALU.mult))
                            own.chain(G.tensor_tensor(sx[:, :], sx[:, :], sqp[:, :], ALU.add))
                    own.restart()
                pool.sem_inc(sx_ready, 1)


def _constants():
    c = np.zeros((P, NK), np.float32)
    r = np.arange(32)
    for a, b in ((0, 0), (1, 1), (2, 1), (3, 0)):
        c[32 * b + r, K_PERM1 + 32 * a + r] = 1
    for a in range(4):
        for b in ((0, 2), (1, 3))[a % 2]:
            c[32 * b + r, K_PERM2 + 32 * a + r] = 1
    c[:, K_ID:K_ID + P] = np.eye(P)
    i = np.arange(P)
    tri = np.where(i[None, :] <= i[:, None], 0.0, -HEAVY)
    c[:, K_AMASK + P:K_AMASK + 2 * P] = tri
    c[:, K_GMASK:K_GMASK + P] = (i[:, None] <= i[None, :]) & (i[:, None] // 64 == i[None, :] // 64)
    t = np.arange(T)
    c[:, K_CMASK:K_CMASK + T] = t % 64 != 0
    c[:, K_IOTA:K_IOTA + T] = t
    f = np.arange(32, dtype=np.float32) / np.float32(32)
    c[:, K_INVF] = np.tile(np.float32(1) / np.float32(10000.0) ** f, 4)
    return c


def _columns(m, width):
    k, n = m.shape
    return m.reshape(k // (2 * P), 2, P, n // width, width).transpose(3, 0, 2, 1, 4)


def _weights(inp, l):
    w = inp["w_in"][l]
    at = np.cumsum([0, BR, BR, QR, KVR, ROPE, BR, 512, 512, BR, 16, BR, BR, BR])
    (s5u, s5g, cq, ckv, kr, mlag, gq, gk, gv, glr, glag, lruu, lrug) = [w[:, a:b] for a, b in zip(at[:-1], at[1:])]
    pad = np.zeros((D, 2 * CC - 256 - ROPE - 16), np.float32)
    tiles = lambda m: m.reshape(D, G8, 1, P)
    gates = np.concatenate([tiles(lrug), tiles(mlag), tiles(glag), tiles(s5g)], axis=2).reshape(D, 4 * BR)
    m = np.concatenate([lruu, s5u, gq, gk, cq, ckv, kr, glr, pad, gv, gates], axis=1)
    o = inp["w_out"][l]
    o = np.concatenate([o[3 * BR:], o[2 * BR:3 * BR], o[BR:2 * BR], o[:BR]], axis=0)
    parts = [_columns(m, CC), _columns(inp["s5_w_glu"][l], CC), _columns(o, CC)]
    return np.concatenate([p.reshape(-1, P, 2, CC) for p in parts])


def _tiles(v):
    return v.reshape(-1, P).T


def kernel(**inputs):
    import concourse.bacc as _bacc
    from concourse.bass_utils import run_bass_kernel_spmd as _run

    inp = {k: np.asarray(v) for k, v in inputs.items()}
    fp = np.float32
    arrays = {}
    arrays["w"] = np.concatenate([_weights(inp, l) for l in range(L)])
    arrays["x"] = np.ascontiguousarray(inp["x"][0].reshape(T, KT, P).transpose(2, 1, 0))
    arrays["pos"] = np.ascontiguousarray(inp["positions"])
    arrays["const"] = _constants()

    small = np.zeros((P, L, NS), fp)
    pg = np.zeros((P, L, G8, NPG_IN), fp)
    s5 = np.zeros((P, L, 3, 32), fp)
    mla = np.zeros((L * G8 + 1, P, CQ * T + 2 * KVR), fp)
    mix = np.zeros((L * G8 + 1, P, 6, P), fp)
    wg2 = np.zeros((L * G8 + 1, 16, P), fp)
    for l in range(L):
        g = lambda name: inp[name][l]
        for a, v in ((S_NORM, g("norm_g")), (S_QG, g("mla_q_norm_g")), (S_KVG, g("mla_kv_norm_g")),
                     (S_BGLU, g("s5_b_glu")), (S_S5G, g("s5_out_g")), (S_FG, inp["final_g"])):
            small[:, l, a:a + v.size // P] = _tiles(v)
        for j in range(4):
            pg[:, l, :, C_CONV + j] = _tiles(g("lru_conv_w")[j])
        for c, v in ((C_CONVB, "lru_conv_b"), (C_BA, "lru_b_a"), (C_BX, "lru_b_x"), (C_LAM, "lru_lambda"),
                     (C_LRUG, "lru_out_g"), (C_MLAG, "mla_out_g"), (C_GLAG, "gla_out_g")):
            pg[:, l, :, c] = _tiles(g(v))
        pg[:, l, :, C_S5D] = _tiles(g("s5_d").reshape(-1))
        for h in range(4):
            pg[:, l, 2 * h, C_GLAB] = pg[:, l, 2 * h + 1, C_GLAB] = g("gla_b_gate")[P * h:P * h + P]
        for a in range(2):
            r = slice(64 * a, 64 * a + 64)
            s5[r, l, 0, :] = g("s5_log_dt")[a::2][None, :]
            s5[r, l, 1, :] = g("s5_lambda_re")[a::2].T
            s5[r, l, 2, :] = g("s5_lambda_im")[a::2].T
        uq = g("mla_w_uq").reshape(CQ, P, G8, 128 + ROPE)
        uk, uv = g("mla_w_uk").reshape(CKV, P, G8, P), g("mla_w_uv").reshape(CKV, P, G8, P)
        for i in range(G8):
            n = l * G8 + i
            q = uq[:, :, i, :].transpose(1, 0, 2)
            q = np.concatenate([q, q[:, :, 160:192], q[:, :, 128:160]], axis=2)
            mla[n, :, 0:CQ * T] = q.reshape(P, CQ * T)
            mla[n, :, CQ * T:CQ * T + KVR] = uk[:, :, i, :].transpose(1, 0, 2).reshape(P, KVR)
            mla[n, :, CQ * T + KVR:] = uv[:, :, i, :].transpose(1, 0, 2).reshape(P, KVR)
            mix[n, :, 0], mix[n, :, 1] = g("lru_w_a")[i], g("lru_w_x")[i]
            wg2[n] = g("gla_w_gate")[:, P * (i // 2):P * (i // 2) + P]
            for j in range(4):
                for a in range(2):
                    grp = 8 * i + 2 * j + a
                    rows, states = slice(32 * j + 16 * a, 32 * j + 16 * a + 16), slice(64 * a, 64 * a + 64)
                    cols = slice(32 * j + 16 * a, 32 * j + 16 * a + 16)
                    mix[n, rows, 2, states] = g("s5_b_re")[grp].T
                    mix[n, rows, 3, states] = g("s5_b_im")[grp].T
                    mix[n, states, 4, cols] = g("s5_c_re")[grp].T
                    mix[n, states, 5, cols] = g("s5_c_im")[grp].T
    arrays.update(small=small, pg=pg, s5raw=s5, mlaw=mla, mixw=mix, wg2=wg2)

    nc = _bacc.Bacc("TRN2", target_bir_lowering=False, num_devices=1, dynamic_dma_scratch_size=1024)
    aps = {k: nc.dram_tensor(f"in_{k}", a.shape, mybir.dt.from_np(a.dtype), kind="ExternalInput").ap()
           for k, a in arrays.items()}
    out = nc.dram_tensor("out", (P, KT, T), mybir.dt.float32, kind="ExternalOutput").ap()
    trunk(nc, *(aps[k] for k in ("w", "x", "pos", "const", "small", "pg", "s5raw", "mlaw", "mixw", "wg2")), out)
    r = _run(nc, [{f"in_{k}": a for k, a in arrays.items()}], core_ids=[0])
    return r.results[0]["out"].transpose(2, 1, 0).reshape(1, T, D)
```

```python
import numpy as np
import concourse.bass as bass
from concourse import mybir
from contextlib import ExitStack

P = 128
L = 2
T = 256
D = 4096
KT = D // P
BR = D // 4
G8 = BR // P
QR, KVR, ROPE = D * 3 // 16, D // 8, 64
CQ, CKV = QR // P, KVR // P
CC = 256
CH_HALF = KT // 2
CH_PAIR = 2 * CH_HALF
CH_GLU = 4
N_PRE, N_V, N_GATE = 0, 9 * CH_PAIR, 11 * CH_PAIR
N_GLU = N_GATE + G8 * CH_PAIR
N_OUT = N_GLU + 4 * CH_GLU
N_LAYER = N_OUT + 8 * CH_PAIR
H_PRE, H_V, H_GATE = 0, 18, 22
H_GLU = H_GATE + 2 * G8
H_OUT = H_GLU + 4
H_LAYER = H_OUT + 16
Y_GLU = {3: 0, 5: 1, 6: 2, 7: 3, 9: 4, 10: 5, 13: 6, 14: 7}
Y_OUT = {0: (8,), 1: (9,), 4: (10,), 5: (11,), 10: (12, 13), 11: (14,), 12: (15,)}
RAW, W2, LOOK = 8, 4, 3
Z_LRU, Z_S5, Z_Q, Z_K, Z_CQ, Z_CKV = 0, 8, 16, 20, 24, 30
NZ = 34
(C_CONV, C_CONVB, C_BA, C_BX, C_LAM, C_LRUG, C_MLAG, C_GLAG, C_GLAB, C_S5D) = (0, 4, 5, 6, 7, 8, 9, 10, 11, 12)
C_SP2, C_HBA, C_HBX, C_F0, C_R, C_SR, C_NSI, C_NSP4, NPG = 13, 14, 15, 16, 20, 24, 28, 32, 33
NPG_IN = 13
K_PERM1, K_PERM2, K_ID, K_AMASK, K_GMASK, K_CMASK, K_IOTA, NK = 0, 128, 256, 384, 640, 768, 1024, 1280
S_NORM, S_QG, S_KVG, S_BGLU, S_S5G, S_FG, S_INVF, NS = 0, 32, 38, 42, 50, 58, 90, 91
EPS = 1e-6
MAGIC = 12582912.0
TWO_PI = 6.283185
SCALE = float(128 + ROPE) ** -0.5
TAU = 16.0
HEAVY = 1.0e30


def trunk(nc, w, x, pos, const, small, pg_in, s5raw, mlaw_d, mixw_d, wg2_d, out):
    F, R, I = mybir.dt.float32, mybir.dt.float32r, mybir.dt.int32
    ACT, ALU, AX = mybir.ActivationFunctionType, mybir.AluOpType, mybir.AxisListType
    ctx = ExitStack()
    with ctx:
        def sb(name, shape, dt=F):
            return ctx.enter_context(nc.sbuf_tensor(name, shape, dt))

        def sem(name):
            return ctx.enter_context(nc.semaphore(name))

        xres = nc.dram_tensor("xres", (P, KT, T), F).ap()

        hb = sb("hb", [P, KT, 2, T], R)
        raw = sb("raw", [P, RAW, 2, CC])
        w2 = sb("w2", [P, W2, 2, 2, CC], R)
        zb = sb("zb", [P, NZ, T])
        kg = sb("kg", [P, T])
        vb = sb("vb", [P, G8, 2, P])
        ymla = sb("ymla", [P, G8, T])
        gs5 = sb("gs5", [P, G8, T])
        half_lo = sb("half_lo", [P, 2, T])
        gate = sb("gate", [P, 2, 2, T])
        kc = sb("kc", [P, NK])
        sm_all = sb("sm_all", [P, L, NS])
        sm = sb("sm", [P, NS])
        pg_all = sb("pg_all", [P, L, G8, NPG_IN])
        pgl = sb("pgl", [P, G8, NPG])
        pg = sb("pg", [P, NPG])
        cst = sb("cst", [P, 4])
        ones = sb("ones", [P, 1])
        rope = sb("rope", [P, T])
        kext = sb("kext", [P, T])
        mlaw = sb("mlaw", [P, CQ * T])
        mixw = sb("mixw", [P, 6, P])
        wg2 = sb("wg2", [P, P])
        cprime = sb("cprime", [P, 2, 4, 32])
        xx = sb("xx", [P, 2, T])
        yy = sb("yy", [P, 2, T])
        g2 = sb("g2", [P, 2, T])
        tab = sb("tab", [P, 3, T])
        nf = sb("nf", [P, T])
        us = sb("us", [P, 2, T], R)
        bhi = sb("bhi", [P, 2, P], R)
        blo = sb("blo", [P, 2, P], R)
        yl = sb("yl", [P, T])
        kv = sb("kv", [P, 2, T])
        prob = sb("prob", [P, 3, P])
        probt = sb("probt", [P, 3, P])
        ym = sb("ym", [P, T])
        row = sb("row", [P, 8])
        ga = sb("ga", [P, T])
        gb = sb("gb", [P, T])
        lg = sb("lg", [P, 2, T])
        qd = sb("qd", [P, T])
        ki = sb("ki", [P, T])
        ke = sb("ke", [P, T])
        attm = sb("attm", [P, 2, P])
        st = sb("st", [P, 3, P])
        tot = sb("tot", [P, 4])
        vs = sb("vs", [P, 2, P])
        yg = sb("yg", [P, T])
        xc = probt[:, 0:2, :].rearrange("p a t -> p (a t)")
        trti = lg[:, :, :]
        cum, ep = lg[:, 0, :], lg[:, 1, :]
        tw, sq, decay = qd[:, :], yg[:, :], ki[:, :]
        qn = st[:, 0:2, :].rearrange("p a t -> p (a t)")
        qr = prob[:, 0:2, :].rearrange("p a t -> p (a t)")
        posi = kext[:, :].bitcast(I)
        ssq = sb("ssq", [P, 6, T])
        sx = sb("sx", [P, T])
        ncol = sb("ncol", [P, 12])
        rcol = sb("rcol", [P, 12])
        s5_all = sb("s5_all", [P, L, 3, 32])
        s5 = gate[:, :, :, :].rearrange("p h a (r b) -> p (h a r) b", b=32)
        lru8 = sb("lru8", [P, 6, G8])
        hf = (xx, yy, g2)

        ps = ctx.enter_context(nc.psum_tensor("ps", [P, 8, 512], F))
        B_BU, B_Y, B_A, B_B = 4, 5, 6, 7

        x_loaded = [sem(f"x_loaded{i}") for i in range(8)]
        const_loaded, pos_loaded, sm_loaded, small_loaded = (sem("const_loaded"), sem("pos_loaded"), sem("sm_loaded"),
                                                             sem("small_loaded"))
        raw_loaded = [sem(f"raw_loaded{i}") for i in range(RAW)]
        qw_loaded, kvw_loaded, mix_loaded, wg2_loaded = (sem("qw_loaded"), sem("kvw_loaded"), sem("mix_loaded"),
                                                        sem("wg2_loaded"))
        xold_loaded, x_stored, out_stored = [sem("xold_loaded0"), sem("xold_loaded1")], sem("x_stored"), sem("out_stored")
        hi_ready, w2_ready, chunk_done = sem("hi_ready"), sem("w2_ready"), sem("chunk_done")
        lo_copied, acc_read = sem("lo_copied"), sem("acc_read")
        squares_made, sx_ready, x_ready = sem("squares_made"), sem("sx_ready"), sem("x_ready")
        hf_ready, h_hi_ready, h_ready = sem("hf_ready"), sem("h_hi_ready"), sem("h_ready")
        cols_ready, rms_ready, rcol_ready, rstd_ready = (sem("cols_ready"), sem("rms_ready"), sem("rcol_ready"),
                                                         sem("rstd_ready"))
        rope_made, consts_made = sem("rope_made"), sem("consts_made")
        kperm_ready, krot_ready, ksum_ready, kext_ready = (sem("kperm_ready"), sem("krot_ready"), sem("ksum_ready"),
                                                           sem("kext_ready"))
        latent_squared, latents_ready = sem("latent_squared"), sem("latents_ready")
        pgl_dve, pgl_act, act_prep, dve_prep = sem("pgl_dve"), sem("pgl_act"), sem("act_prep"), sem("dve_prep")
        iter_done, pg_ready, us_ready, vs_ready = sem("iter_done"), sem("pg_ready"), sem("us_ready"), sem("vs_ready")
        cprime_ready, nf_ready, tab_ready = sem("cprime_ready"), sem("nf_ready"), sem("tab_ready")
        bu_ready, bu_read, tab_used, state_ready, state_used = (sem("bu_ready"), sem("bu_read"), sem("tab_used"),
                                                                sem("state_ready"), sem("state_used"))
        xc_ready, ri_ready, lru_act, yl_ready, yl_squared = (sem("xc_ready"), sem("ri_ready"), sem("lru_act"),
                                                             sem("yl_ready"), sem("yl_squared"))
        q_ready, qn_ready, qr_ready, kv_ready, kv_copied = (sem("q_ready"), sem("qn_ready"), sem("qr_ready"),
                                                            sem("kv_ready"), sem("kv_copied"))
        sc_ready, max_ready, prob_ready, probn_ready = (sem("sc_ready"), sem("max_ready"), sem("prob_ready"),
                                                        sem("probn_ready"))
        pt_ready, pt_copied, o_ready, ym_ready, ym_squared = (sem("pt_ready"), sem("pt_copied"), sem("o_ready"),
                                                              sem("ym_ready"), sem("ym_squared"))
        la_ready, la_abs, la_act, cum_ready, decays_ready = (sem("la_ready"), sem("la_abs"), sem("la_act"),
                                                             sem("cum_ready"), sem("decays_ready"))
        qk_ready, att_ready, ket_copied, att_masked = (sem("qk_ready"), sem("att_ready"), sem("ket_copied"),
                                                       sem("att_masked"))
        kvs_ready, st_ready, og_ready, yg_ready, yg_squared = (sem("kvs_ready"), sem("st_ready"), sem("og_ready"),
                                                               sem("yg_ready"), sem("yg_squared"))
        silu_ready, glu_ready, glu_tanh, glu_squared, y2_ready = (
            sem("silu_ready"), sem("glu_ready"), sem("glu_tanh"), sem("glu_squared"), sem("y2_ready"))
        us_split = sem("us_split")
        x_added, x_saved = sem("x_added"), sem("x_saved")
        y2_squared, last_squared = sem("y2_squared"), sem("last_squared")
        scanned, back_ready = sem("scanned"), sem("back_ready")
        xc_begun = sem("xc_begun")
        gelu_done, outx_ready, outx, gla_exp = sem("gelu_done"), sem("outx_ready"), sem("outx"), sem("gla_exp")
        act_own, dve_own, pool_own = sem("act_own"), sem("dve_own"), sem("pool_own")
        block = ctx.enter_context(nc.Block())

        class Own:

            def __init__(self, eng, s):
                self.eng, self.s, self.n = eng, s, 0

            def do(self, ins):
                ins.then_inc(self.s, 1)
                self.n += 1

            def wait(self):
                self.eng.wait_ge(self.s, self.n)

            def chain(self, ins):
                self.do(ins)
                self.wait()

            def pause(self):
                self.eng.sem_inc(self.s, 1)
                self.n += 1

            def restart(self):
                if self.n:
                    self.pause()
                    self.wait()
                    self.eng.sem_clear(self.s)
                    self.n = 0

        @block.sync
        def _(sp):
            sp.dma_start(posi[:, :], pos.partition_broadcast(P)).then_inc(pos_loaded, 16)
            sp.dma_start(sm_all[:, :, :], small).then_inc(sm_loaded, 16)
            for i in range(8):
                sp.dma_start(zb[:, 4 * i:4 * i + 4, :], x[:, 4 * i:4 * i + 4, :]).then_inc(x_loaded[i], 16)
            sp.dma_start(kc[:, :], const).then_inc(const_loaded, 16)
            for s in range(RAW):
                sp.dma_start(raw[:, s], w[s]).then_inc(raw_loaded[s], 16)
            sp.dma_start(pg_all[:, :, :, :], pg_in).then_inc(small_loaded, 16)
            sp.dma_start(s5_all[:, :, :, :], s5raw).then_inc(small_loaded, 16)
            sp.dma_start(mlaw[:, :], mlaw_d[0, :, 0:CQ * T]).then_inc(qw_loaded, 16)
            sp.dma_start(mixw[:, :, :], mixw_d[0]).then_inc(mix_loaded, 16)
            sp.dma_start(wg2[64:80, :], wg2_d[0]).then_inc(wg2_loaded, 16)

            def round_of_loads(q):
                for s in range(RAW):
                    sp.wait_ge(w2_ready, q * RAW + s + 1)
                    sp.dma_start(raw[:, s], w[q * RAW + (RAW + s)]).then_inc(raw_loaded[s], 16)

            for i in range(4):
                with sp.Fori(2 * i, 2 * i + 2) as q:
                    round_of_loads(q)
                sp.dma_start(xres[:, 8 * i:8 * i + 8, :], x[:, 8 * i:8 * i + 8, :]).then_inc(x_saved, 16)
            with sp.Fori(8, L * N_LAYER // RAW - 1) as q:
                round_of_loads(q)
            for s in range(LOOK):
                sp.wait_ge(w2_ready, L * N_LAYER - RAW + s + 1)
                sp.dma_start(raw[:, s], w[s]).then_inc(raw_loaded[s], 16)
            for i in range(4):
                sp.wait_ge(outx_ready, i + 1)
                sp.dma_start(out[:, 8 * i:8 * i + 8, :], zb[:, 8 * i:8 * i + 8, :]).then_inc(out_stored, 16)
            sp.wait_ge(out_stored, 64)
            sp.wait_ge(x_saved, 64)
            sp.wait_ge(x_stored, 16 * (1 + 16 * L))

        @block.tensor
        def _(pe):
            mm = nc.tensor.matmul

            def chunk(n0, c, half, tokens=False, tiles=(0, 1), k0=0, nk=KT):
                kcs = 2 * (c % (nk // 2))
                pe.wait_ge(w2_ready, n0 + (c + 1))
                for kk in range(2):
                    k = kcs + kk
                    for j in tiles:
                        acc = ps[:, 2 * half + j, :]
                        s = c % W2
                        if tokens:
                            a_hi, a_lo = hb[:, k0 + k, 0, P * j:P * j + P], hb[:, k0 + k, 1, P * j:P * j + P]
                            m_both, m_hi = w2[:, s, kk, :, :].rearrange("p a c -> p (a c)"), w2[:, s, kk, 0, :]
                        else:
                            a_hi, a_lo = w2[:, s, kk, 0, P * j:P * j + P], w2[:, s, kk, 1, P * j:P * j + P]
                            m_both, m_hi = hb[:, k0 + k, :, :].rearrange("p a c -> p (a c)"), hb[:, k0 + k, 0, :]
                        if k > 0:
                            mm(acc[:, T:], a_lo, m_hi, start=False, stop=False, skip_group_check=True)
                        last = mm(acc, a_hi, m_both, start=(k == 0), stop=(k == nk - 1), skip_group_check=True)
                        if k == 0:
                            last = mm(acc[:, T:], a_lo, m_hi, start=False, stop=False, skip_group_check=True)
                last.then_inc(chunk_done, 1)

            def columns(sums):
                for i, tiles in enumerate(sums):
                    for b in range(2):
                        for n, s in enumerate(tiles):
                            last = mm(ps[:, B_Y, 2 * i + b:2 * i + b + 1], s[:, P * b:P * b + P], ones[:, :],
                                      start=(n == 0), stop=(n == len(tiles) - 1))
                last.then_inc(cols_ready, 1)

            def spread(dsts, count):
                pe.wait_ge(rcol_ready, count)
                for i, d in enumerate(dsts):
                    for b in range(2):
                        last = mm(d[:, P * b:P * b + P], rcol[:, 2 * i + b:2 * i + b + 1].to_broadcast([P, P]),
                                  kc[:, K_ID:K_ID + P], start=True, stop=True)
                last.then_inc(rstd_ready, 1)

            pe.sem_inc(chunk_done, W2)
            pe.sem_inc(state_used, 1)
            pe.wait_ge(const_loaded, 16)
            pe.wait_ge(consts_made, 1)

            with pe.Fori(0, L) as l:
                n_l, h_l, c_l = l * N_LAYER, l * H_LAYER, l * 4
                pe.wait_ge(sx_ready, l + 1)
                pe.wait_ge(last_squared, l + 1)
                columns([(sx, ssq[:, 0, :], ssq[:, 1, :])])
                spread([ps[:, B_BU, 0:T]], c_l + 1)
                for c in range(CH_PAIR):
                    if c % CH_HALF == 0:
                        pe.wait_ge(acc_read, h_l + c // CH_HALF + 1)
                    if c < CH_HALF:
                        pe.wait_ge(h_ready, l * 32 + (c + 1))
                    chunk(n_l, c, c // CH_HALF)
                with pe.Fori(1, 8) as i:
                    n0, h0 = n_l + i * CH_PAIR, h_l + i * 2
                    for c in range(CH_PAIR):
                        if c % CH_HALF == 0:
                            pe.wait_ge(acc_read, h0 + (c // CH_HALF + 1))
                        chunk(n0, c, c // CH_HALF)
                for c in range(CH_PAIR):
                    if c % CH_HALF == 0:
                        pe.wait_ge(acc_read, h_l + (16 + c // CH_HALF + 1))
                    chunk(n_l + 8 * CH_PAIR, c, c // CH_HALF, tiles=(0, 1) if c < CH_HALF else (0,))
                for c in range(2 * CH_PAIR):
                    if c % CH_HALF == 0:
                        pe.wait_ge(acc_read, h_l + (H_V + c // CH_HALF + 1))
                    chunk(n_l + N_V, c, (c // CH_HALF) % 2, tokens=True)
                    if c == 3:
                        pe.wait_ge(acc_read, h_l + H_V + 2)
                        mm(ps[:, B_A, 0:T], kc[0:ROPE, K_PERM1:K_PERM1 + P], kg[0:ROPE, :], start=True,
                           stop=True).then_inc(kperm_ready, 1)
                    if c == 6:
                        pe.wait_ge(krot_ready, l + 1)
                        mm(ps[:, B_A, 0:T], kc[:, K_PERM2:K_PERM2 + P], qr[:, :], start=True,
                           stop=True).then_inc(ksum_ready, 1)
                    if c == 20:
                        pe.wait_ge(latent_squared, 10 * l + 10)
                        columns([(ssq[:, 2, :],), (ssq[:, 3, :],)])
                    if c == 23:
                        spread([ps[:, B_B, 0:T], ps[:, B_B, T:]], c_l + 2)

                with pe.Fori(0, G8) as g:
                    it = l * G8 + g
                    n0, h0 = n_l + N_GATE + g * CH_PAIR, h_l + H_GATE + g * 2

                    def s5_in(j):
                        if j == 0:
                            pe.wait_ge(us_split, it * 2 + 2)
                        pe.wait_ge(bu_read, it * 4 + (j + 1))
                        r = slice(32 * j, 32 * j + 32)
                        for a in range(2):
                            o = ps[:, B_BU, T * a:T * a + T]
                            mm(o, bhi[r, a, :], us[r, 0, :], start=True, stop=False)
                            mm(o, bhi[r, a, :], us[r, 1, :], start=False, stop=False)
                            last = mm(o, blo[r, a, :], us[r, 0, :], start=False, stop=True)
                        last.then_inc(bu_ready, 1)

                    def s5_out(j):
                        if j == 0:
                            pe.wait_ge(cprime_ready, it + 1)
                            pe.wait_ge(iter_done, it + 1)
                        pe.wait_ge(state_ready, it * 4 + (j + 1))
                        o = ps[32 * j:32 * j + 32, B_Y, 0:T]
                        mm(o, cprime[:, 0, j, :], xx[:, 0, :], start=True, stop=False)
                        mm(o, cprime[:, 1, j, :], xx[:, 1, :], start=False, stop=True).then_inc(state_used, 1)

                    def lru_gates():
                        pe.wait_ge(xc_ready, it + 1)
                        pe.wait_ge(mix_loaded, it * 16 + 16)
                        pe.wait_ge(st_ready, it + 1)
                        mm(ps[:, B_B, 0:T], mixw[:, 0, :], xc[:, :], start=True, stop=True)
                        mm(ps[:, B_B, T:], mixw[:, 1, :], xc[:, :], start=True, stop=True).then_inc(ri_ready, 1)

                    def mla_q():
                        pe.wait_ge(qw_loaded, it * 16 + 16)
                        pe.wait_ge(latents_ready, 10 * l + 10)
                        pe.wait_ge(yg_ready, it + 1)
                        for part in range(2):
                            for k in range(CQ):
                                last = mm(ps[:, B_A, T * part:T * part + T],
                                          mlaw[:, T * k + P * part:T * k + P * part + P], zb[:, Z_CQ + k, :],
                                          start=(k == 0), stop=(k == CQ - 1))
                        last.then_inc(q_ready, 1)

                    def mla_kv():
                        pe.wait_ge(kvw_loaded, it * 16 + 16)
                        pe.wait_ge(qr_ready, it + 1)
                        for k in range(CKV):
                            mm(ps[:, B_A, 0:T], mlaw[:, P * k:P * k + P], zb[:, Z_CKV + k, :],
                               start=(k == 0), stop=(k == CKV - 1))
                        for b in range(2):
                            for k in range(CKV):
                                last = mm(ps[:, B_A, T + P * b:T + P * b + P], zb[:, Z_CKV + k, P * b:P * b + P],
                                          mlaw[:, KVR + P * k:KVR + P * k + P], start=(k == 0), stop=(k == CKV - 1))
                        last.then_inc(kv_ready, 1)

                    def mla_scores():
                        pe.wait_ge(kv_copied, it + 1)
                        for b in range(2):
                            o = ps[:, B_A, P * b:P * b + P * (b + 1)]
                            mm(o, qn[:, P * b:P * b + P], kv[:, 0, 0:P * (b + 1)], start=True, stop=False)
                            last = mm(o, qr[:, P * b:P * b + P], kext[:, 0:P * (b + 1)], start=False, stop=True)
                        last.then_inc(sc_ready, 1)

                    def mla_turn():
                        pe.wait_ge(probn_ready, it + 1)
                        for b in range(3):
                            last = nc.tensor.transpose(ps[:, B_A, P * b:P * b + P], prob[:, b, :], kc[:, K_ID:K_ID + P])
                        last.then_inc(pt_ready, 1)

                    def mla_out():
                        pe.wait_ge(pt_copied, it + 1)
                        mm(ps[:, B_A, 0:P], kv[:, 1, 0:P], probt[:, 0, :], start=True, stop=True)
                        mm(ps[:, B_A, P:T], kv[:, 1, 0:P], probt[:, 1, :], start=True, stop=False)
                        mm(ps[:, B_A, P:T], kv[:, 1, P:T], probt[:, 2, :], start=False, stop=True).then_inc(o_ready, 1)

                    def gla_gate():
                        pe.wait_ge(wg2_loaded, it * 16 + 16)
                        pe.wait_ge(lru_act, it + 2)
                        mm(ps[:, B_B, 0:T], wg2[64:80, :], kg[64:80, :], start=True, stop=True).then_inc(la_ready, 1)

                    def gla_scores():
                        pe.wait_ge(qk_ready, it + 1)
                        pe.wait_ge(ym_ready, it + 2)
                        for b in range(2):
                            mm(ps[:, B_A, P * b:P * b + P], ki[:, P * b:P * b + P], qd[:, P * b:P * b + P],
                               start=True, stop=True)
                        for b in range(2):
                            last = nc.tensor.transpose(ps[:, B_A, T + P * b:T + P * b + P], ke[:, P * b:P * b + P],
                                                       kc[:, K_ID:K_ID + P])
                        last.then_inc(att_ready, 1)

                    def gla_states():
                        pe.wait_ge(ket_copied, it + 1)
                        pe.wait_ge(cum_ready, it + 1)
                        pe.wait_ge(vs_ready, it + 1)
                        mm(ps[:, B_B, 0:P], probt[0:64, 0, :], vs[0:64, 0, :], start=True, stop=True)
                        mm(ps[:, B_B, 2 * P:3 * P], probt[0:64, 1, :], vs[0:64, 1, :], start=True,
                           stop=True).then_inc(kvs_ready, 1)

                    def gla_states2():
                        pe.wait_ge(kvs_ready, it * 2 + 1)
                        mm(ps[:, B_B, P:2 * P], probt[64:128, 0, :], vs[64:128, 0, :], start=True,
                           stop=True).then_inc(kvs_ready, 1)

                    def gla_out():
                        pe.wait_ge(att_masked, it + 1)
                        pe.wait_ge(st_ready, it + 2)
                        for b in range(2):
                            mm(ps[:, B_A, P * b:P * b + P], vs[:, b, :], attm[:, b, :], start=True, stop=True)
                            for c in (1,) if b == 0 else (2, 3):
                                r = slice(64 * c, 64 * c + 64)
                                last = mm(ps[:, B_A, r], st[:, c - 1, :], qd[:, r], start=False, stop=True,
                                          skip_group_check=True)
                        last.then_inc(og_ready, 1)

                    steps = {0: [mla_q], 1: [lambda: s5_in(0)], 3: [lru_gates], 5: [mla_kv],
                             6: [lambda: s5_in(1)], 7: [mla_scores], 8: [gla_gate], 10: [lambda: s5_out(0)],
                             14: [lambda: s5_in(2)], 17: [mla_turn], 18: [lambda: s5_out(1)], 20: [mla_out],
                             22: [gla_scores, lambda: s5_in(3)], 25: [gla_states, lambda: s5_out(2), gla_states2],
                             29: [gla_out], 31: [lambda: s5_out(3)]}
                    for c in range(CH_PAIR):
                        if c % CH_HALF == 0:
                            pe.wait_ge(acc_read, h0 + (c // CH_HALF + 1))
                        chunk(n0, c, c // CH_HALF)
                        for step in steps.get(c, ()):
                            step()

                pe.wait_ge(iter_done, l * G8 + (G8 + 1))
                pe.wait_ge(yg_squared, l * G8 + G8)
                columns([(ssq[:, i, :],) for i in range(6)])
                for c in range(4 * CH_GLU):
                    if c % CH_GLU == 0:
                        pe.wait_ge(acc_read, h_l + (H_GLU + c // CH_GLU + 1))
                    if c < CH_GLU:
                        pe.wait_ge(glu_ready, l * 4 + (c + 1))
                    if c == 2:
                        spread([ps[:, B_BU, 0:T], ps[:, B_BU, T:], ps[:, B_A, 0:T], ps[:, B_A, T:],
                                ps[:, B_B, 0:T], ps[:, B_B, T:]], c_l + 3)
                    chunk(n_l + N_GLU, c, (c // CH_GLU) % 2, k0=24, nk=8)
                for c in range(CH_PAIR):
                    if c % CH_HALF == 0:
                        pe.wait_ge(acc_read, h_l + (H_OUT + c // CH_HALF + 1))
                    if c == 6:
                        pe.wait_ge(glu_squared, l * 4 + 4)
                        columns([(sx,)])
                    if c == 9:
                        spread([ps[:, B_Y, 0:T]], c_l + 4)
                    if c < CH_HALF:
                        pe.wait_ge(h_ready, l * 32 + (16 + c + 1))
                    chunk(n_l + N_OUT, c, c // CH_HALF)
                with pe.Fori(1, 8) as i:
                    n0, h0 = n_l + N_OUT + i * CH_PAIR, h_l + H_OUT + i * 2
                    for c in range(CH_PAIR):
                        if c % CH_HALF == 0:
                            pe.wait_ge(acc_read, h0 + (c // CH_HALF + 1))
                        chunk(n0, c, c // CH_HALF)
            pe.wait_ge(sx_ready, L + 1)
            pe.wait_ge(last_squared, L + 1)
            columns([(sx, ssq[:, 0, :], ssq[:, 1, :])])
            spread([ps[:, B_BU, 0:T]], 4 * L + 1)

        @block.scalar
        def _(act):
            own = Own(act, act_own)
            A = nc.scalar.activation
            EPS1, EPS4, HALF_PI, ONE = cst[:, 0:1], cst[:, 1:2], cst[:, 2:3], cst[:, 3:4]

            def hi(n0, c):
                s, d = (c + LOOK) % RAW, (c + LOOK) % W2
                act.wait_ge(raw_loaded[s], n0 * (16 // RAW) + 16 * ((c + LOOK) // RAW + 1))
                act.wait_ge(chunk_done, n0 + (c + LOOK + 1))
                A(w2[:, d, :, 0, :], raw[:, s, :, :], ACT.Copy).then_inc(hi_ready, 1)

            def evac(h0, half, n_done, tiles=2):
                act.wait_ge(chunk_done, n_done + W2)
                act.wait_ge(acc_read, h0 + 2)
                A(half_lo[:, 0:tiles, :], ps[:, 2 * half:2 * half + tiles, 0:T], ACT.Copy).then_inc(lo_copied, 1)

            def rms(count, cols, n, eps):
                act.wait_ge(cols_ready, count)
                A(ncol[:, 0:cols], ps[:, B_Y, 0:cols], ACT.Sqrt, bias=eps, scale=1.0 / n).then_inc(rms_ready, 1)

            def split_hi(k, count):
                act.wait_ge(hf_ready, count)
                A(hb[:, 2 * k:2 * k + 2, 0, :], hf[k % 3][:, :, :], ACT.Copy).then_inc(h_hi_ready, 1)

            for i in range(8):
                act.wait_ge(x_loaded[i], 16)
                if i >= 2:
                    act.wait_ge(x_ready, i - 1)
                A(gs5[:, 4 * (i % 2):4 * (i % 2) + 4, :], zb[:, 4 * i:4 * i + 4, :], ACT.Square).then_inc(squares_made, 1)
                if i == 1:
                    act.wait_ge(consts_made, 1)
                    act.wait_ge(rope_made, 1)
                    A(gb[0:64, :], ga[0:64, :], ACT.Abs).then_inc(act_prep, 1)
                    act.wait_ge(act_prep, 1)
                    A(rope[0:64, :], gb[0:64, :], ACT.Sin, bias=HALF_PI[0:64], scale=-1.0).then_inc(act_prep, 1)
                    A(rope[64:96, :], ga[64:96, :], ACT.Sin, scale=-1.0).then_inc(act_prep, 1)
                    A(rope[96:128, :], ga[96:128, :], ACT.Sin).then_inc(act_prep, 1)
            for s in range(LOOK):
                act.wait_ge(raw_loaded[s], 16)
                act.wait_ge(chunk_done, s + 1)
                A(w2[:, s, :, 0, :], raw[:, s, :, :], ACT.Copy).then_inc(hi_ready, 1)
            act.sem_inc(x_stored, 16)
            act.sem_inc(yg_ready, 1)
            act.sem_inc(ym_ready, 1)
            act.sem_inc(lru_act, 1)
            act.sem_inc(tab_ready, 1)

            with act.Fori(0, L) as l:
                n_l, h_l, c_l = l * N_LAYER, l * H_LAYER, l * 4
                rms(c_l + 1, 2, D, EPS1)
                split_hi(0, l * 32 + 1)
                split_hi(1, l * 32 + 2)
                for c in range(CH_PAIR):
                    hi(n_l, c)
                    if c + 2 < CH_HALF:
                        split_hi(c + 2, l * 32 + (c + 3))
                    if c % CH_HALF == CH_HALF - 1:
                        evac(h_l + c // CH_HALF, c // CH_HALF, n_l + (c + 1))
                with act.Fori(1, 8) as i:
                    n0, h0 = n_l + i * CH_PAIR, h_l + i * 2
                    for c in range(CH_PAIR):
                        hi(n0, c)
                        if c % CH_HALF == CH_HALF - 1:
                            evac(h0 + c // CH_HALF, c // CH_HALF, n0 + (c + 1))
                for c in range(CH_PAIR):
                    hi(n_l + 8 * CH_PAIR, c)
                    if c % CH_HALF == CH_HALF - 1:
                        evac(h_l + (16 + c // CH_HALF), c // CH_HALF, n_l + (8 * CH_PAIR + c + 1), 2 - c // CH_HALF)
                for c in range(2 * CH_PAIR):
                    hi(n_l + N_V, c)
                    if c % CH_HALF == CH_HALF - 1:
                        evac(h_l + (H_V + c // CH_HALF), (c // CH_HALF) % 2, n_l + (N_V + c + 1))
                    if c == 21:
                        act.wait_ge(cols_ready, c_l + 2)
                        A(ncol[:, 0:2], ps[:, B_Y, 0:2], ACT.Sqrt, bias=EPS1, scale=1.0 / QR)
                        A(ncol[:, 2:4], ps[:, B_Y, 2:4], ACT.Sqrt, bias=EPS1, scale=1.0 / KVR).then_inc(rms_ready, 1)
                    if c == 10:
                        act.wait_ge(pgl_dve, 3 * l + 1)
                        A(lru8[:, 1, :], lru8[:, 0, :], ACT.Exp, scale=-1.0).then_inc(pgl_act, 1)
                    if c == 34:
                        act.wait_ge(pgl_dve, 3 * l + 3)
                        A(s5[:, 8, :], s5[:, 7, :], ACT.Sin, scale=TWO_PI)
                        A(s5[:, 9, :], s5[:, 7, :], ACT.Sin, scale=TWO_PI / 2).then_inc(pgl_act, 1)

                with act.Fori(0, G8) as g:
                    it = l * G8 + g
                    n0, h0 = n_l + N_GATE + g * CH_PAIR, h_l + H_GATE + g * 2

                    def silu_set():
                        nc.scalar.preload_act_table_set("silu_and_others")

                    def tables(j):
                        act.wait_ge(nf_ready, it * 4 + (j + 1))
                        act.wait_ge(tab_used, it * 4 + (j + 1))
                        act.wait_ge(back_ready, it * 4 + (j + 1))
                        own.do(A(tab[:, 0, :], nf[:, :], ACT.Abs))
                        own.do(A(tab[:, 1, :], nf[:, :], ACT.Sin, scale=TWO_PI))
                        own.do(A(tab[:, 2, :], nf[:, :], ACT.Sin, scale=-TWO_PI))
                        own.wait()
                        A(tab[:, 0, :], tab[:, 0, :], ACT.Sin, bias=HALF_PI, scale=-TWO_PI).then_inc(tab_ready, 1)

                    def lru_tanh():
                        act.wait_ge(ri_ready, it + 1)
                        act.wait_ge(yl_ready, it + 1)
                        own.do(A(trti[:, 0, :], ps[:, B_B, 0:T], ACT.Tanh, bias=pg[:, C_HBA:C_HBA + 1], scale=0.5))
                        A(trti[:, 1, :], ps[:, B_B, T:], ACT.Tanh, bias=pg[:, C_HBX:C_HBX + 1],
                          scale=0.5).then_inc(lru_act, 1)
                        own.wait()
                        own.do(A(tw[:, :], trti[:, 0, :], ACT.Tanh, bias=pg[:, C_SP2:C_SP2 + 1],
                                 scale=pg[:, C_SP2:C_SP2 + 1]))

                    def lru_root():
                        own.wait()
                        own.do(A(sq[:, :], tw[:, :], ACT.Sqrt))

                    def lru_exp():
                        own.wait()
                        A(decay[:, :], trti[:, 0, :], ACT.Exp, bias=pg[:, C_NSP4:C_NSP4 + 1],
                          scale=pg[:, C_NSP4:C_NSP4 + 1]).then_inc(decays_ready, 1)

                    def mla_q():
                        act.wait_ge(q_ready, it + 1)
                        A(qn[:, :], ps[:, B_A, 0:T], ACT.Copy).then_inc(qn_ready, 1)
                        act.dma_start(mlaw[:, 0:2 * KVR], mlaw_d[it, :, CQ * T:]).then_inc(kvw_loaded, 16)

                    def mla_kv():
                        act.wait_ge(kv_ready, it + 1)
                        A(kv[:, :, :].rearrange("p a t -> p (a t)"), ps[:, B_A, :], ACT.Copy).then_inc(kv_copied, 1)
                        act.dma_start(mlaw[:, :], mlaw_d[it + 1, :, 0:CQ * T]).then_inc(qw_loaded, 16)

                    def mla_exp():
                        act.wait_ge(max_ready, it + 1)
                        own.do(A(prob[:, 0, :], prob[:, 0, :], ACT.Exp, bias=row[:, 2:3], scale=SCALE,
                                 accum_out=row[:, 4:5]))
                        A(prob[:, 1:3, :], prob[:, 1:3, :], ACT.Exp, bias=row[:, 3:4], scale=SCALE,
                          accum_out=row[:, 5:6]).then_inc(prob_ready, 1)

                    def mla_turn():
                        act.wait_ge(pt_ready, it + 1)
                        A(probt[:, :, :].rearrange("p a t -> p (a t)"), ps[:, B_A, 0:3 * P], ACT.Copy).then_inc(pt_copied, 1)

                    def mla_out():
                        act.wait_ge(o_ready, it + 1)
                        act.wait_ge(iter_done, it + 1)
                        A(ym[:, :], ps[:, B_A, 0:T], ACT.Copy).then_inc(ym_ready, 1)

                    def exp_set():
                        nc.scalar.preload_act_table_set("natural_log_exp_and_others")

                    def gla_gate():
                        act.wait_ge(la_ready, it + 1)
                        A(ga[:, :], ps[:, B_B, 0:T], ACT.Abs, bias=pg[:, C_GLAB:C_GLAB + 1]).then_inc(la_abs, 1)
                        act.wait_ge(la_abs, it + 1)
                        own.do(A(gb[:, :], ga[:, :], ACT.Exp, scale=-1.0))

                    def gla_ln():
                        own.wait()
                        A(gb[:, :], gb[:, :], ACT.Ln, bias=ONE).then_inc(la_act, 1)

                    def gla_decays():
                        act.wait_ge(cum_ready, it + 1)
                        own.do(A(ep[:, :], cum[:, :], ACT.Exp, scale=1.0 / TAU))
                        own.do(A(ga[:, :], cum[:, :], ACT.Exp, scale=-1.0 / TAU))

                    def gla_rest(chunks):
                        for c in chunks:
                            r = slice(64 * c, 64 * c + 64)
                            last = A(gb[:, r], cum[:, r], ACT.Exp, bias=tot[:, c:c + 1], scale=-1.0 / TAU)
                            if c < 3:
                                own.do(last)
                            else:
                                last.then_inc(gla_exp, 1)

                    def gla_turn():
                        act.wait_ge(att_ready, it + 1)
                        A(probt[:, 0:2, :].rearrange("p a t -> p (a t)"), ps[:, B_A, T:], ACT.Copy).then_inc(ket_copied, 1)

                    def gla_out():
                        act.wait_ge(og_ready, it + 1)
                        act.wait_ge(iter_done, it + 1)
                        A(yg[:, :], ps[:, B_A, 0:T], ACT.Copy).then_inc(yg_ready, 1)

                    def next_mix():
                        act.wait_ge(bu_ready, it * 4 + 4)
                        act.wait_ge(cprime_ready, it + 1)
                        act.dma_start(mixw[:, :, :], mixw_d[it + 1]).then_inc(mix_loaded, 16)
                        act.dma_start(wg2[64:80, :], wg2_d[it + 1]).then_inc(wg2_loaded, 16)

                    def inputs():
                        act.wait_ge(iter_done, it + 1)
                        act.wait_ge(pg_ready, it + 1)
                        A(us[:, 0, :], zb[:, g + Z_S5, :], ACT.Copy).then_inc(us_ready, 1)
                        act.wait_ge(mix_loaded, it * 16 + 16)
                        A(bhi[:, :, :], mixw[:, 2:4, :], ACT.Copy).then_inc(us_ready, 1)
                        A(xc[:, :], zb[:, g, :], ACT.Identity, bias=pg[:, C_CONVB:C_CONVB + 1],
                          scale=pg[:, C_CONV + 3:C_CONV + 4]).then_inc(xc_begun, 1)

                    def first_gates():
                        evac(h0, 0, n0 + CH_HALF)

                    def first_silu():
                        act.wait_ge(acc_read, h0 + 3)
                        A(gate[:, 0, :, :], gate[:, 0, :, :], ACT.Silu).then_inc(silu_ready, 1)

                    silu_set()
                    steps = {0: [inputs], 1: [lambda: tables(0)], 2: [mla_q], 4: [lru_tanh], 6: [mla_kv],
                             8: [lambda: tables(1)], 9: [lru_root], 10: [exp_set, gla_gate], 11: [lru_exp, gla_ln],
                             12: [mla_exp],
                             14: [gla_decays], 15: [lambda: gla_rest((0, 1))], 16: [lambda: gla_rest((2, 3))], 17: [silu_set, lambda: tables(2)], 18: [mla_turn],
                             19: [first_gates], 20: [first_silu], 21: [mla_out], 23: [gla_turn, lambda: tables(3)],
                             26: [next_mix], 30: [gla_out]}
                    for c in range(CH_PAIR):
                        hi(n0, c)
                        for step in steps.get(c, ()):
                            step()
                    evac(h0 + 1, 1, n0 + CH_PAIR)
                    act.wait_ge(acc_read, h0 + 4)
                    A(gate[:, 1, 0, :], gate[:, 1, 0, :], ACT.Silu).then_inc(silu_ready, 1)
                    own.do(A(gs5[:, g, :], gate[:, 1, 1, :], ACT.Silu))
                    own.restart()

                act.wait_ge(iter_done, l * G8 + (G8 + 1))
                act.wait_ge(chunk_done, n_l + (N_GLU + W2))
                for q in range(4):
                    z = zb[:, Z_S5 + 2 * q:Z_S5 + 2 * q + 2, :]
                    own.chain(A(z, z, ACT.Gelu_apprx_tanh))
                    A(hb[:, 24 + 2 * q:26 + 2 * q, 0, :], z, ACT.Copy).then_inc(gelu_done, 1)
                act.wait_ge(cols_ready, c_l + 3)
                A(ncol[:, 0:4], ps[:, B_Y, 0:4], ACT.Sqrt, bias=EPS1, scale=1.0 / BR)
                A(ncol[:, 4:12], ps[:, B_Y, 4:12], ACT.Sqrt, bias=EPS1, scale=1.0 / (BR // 4)).then_inc(rms_ready, 1)
                def glu_evac(m):
                    evac(h_l + (H_GLU + m), m % 2, n_l + (N_GLU + CH_GLU * (m + 1)))

                def glu_act(m):
                    act.wait_ge(acc_read, h_l + (H_GLU + m + 3))
                    own.do(A(gate[:, m % 2, 0, :], gate[:, m % 2, 0, :], ACT.Tanh,
                             bias=lru8[:, 5, 2 * m:2 * m + 1], scale=0.5))
                    A(gate[:, m % 2, 1, :], gate[:, m % 2, 1, :], ACT.Tanh,
                      bias=lru8[:, 5, 2 * m + 1:2 * m + 2], scale=0.5).then_inc(glu_tanh, 1)

                def glu_square(m):
                    act.wait_ge(y2_ready, l * 4 + (m + 1))
                    act.wait_ge(cols_ready, c_l + 3)
                    if m >= 2:
                        act.wait_ge(glu_squared, l * 4 + (m - 1))
                    A(ssq[:, 2 * (m % 2):2 * (m % 2) + 2, :], zb[:, Z_S5 + 2 * m:Z_S5 + 2 * m + 2, :],
                      ACT.Square).then_inc(y2_squared, 1)

                for c in range(4 * CH_GLU):
                    hi(n_l + N_GLU, c)
                    if c >= CH_GLU and c % CH_GLU == 0:
                        glu_evac(c // CH_GLU - 1)
                    if c >= CH_GLU and c % CH_GLU == 1:
                        glu_act(c // CH_GLU - 1)
                    if c >= CH_GLU and c % CH_GLU == 3:
                        glu_square(c // CH_GLU - 1)
                    if c - 1 in Y_GLU:
                        split_hi(Y_GLU[c - 1], l * 32 + (16 + Y_GLU[c - 1] + 1))

                def old_x(h, k):
                    act.dma_start(gate[:, h, :, :], xres[:, k, :]).then_inc(xold_loaded[h], 16)

                def out_evac(i, h):
                    evac(h_l + H_OUT + (i * 2 + h), h, n_l + N_OUT + (i * CH_PAIR + CH_HALF * (h + 1)))

                def out_store(i, h, more):
                    act.wait_ge(outx, l * 16 + (i * 2 + (h + 1)))
                    act.dma_start(xres[:, bass.ds(i * 4 + 2 * h, 2), :], zb[:, bass.ds(i * 4 + 2 * h, 2), :]).then_inc(x_stored, 16)
                    if more:
                        old_x(h, bass.ds(i * 4 + (4 + 2 * h), 2))

                for c in range(CH_PAIR):
                    hi(n_l + N_OUT, c)
                    if c == 0:
                        glu_evac(3)
                    if c == 1:
                        glu_act(3)
                    if c == 4:
                        act.wait_ge(x_saved, 64)
                        act.wait_ge(x_stored, 16 * (16 * l + 1))
                        act.wait_ge(y2_ready, 4 * l + 4)
                        for h in range(2):
                            old_x(h, slice(2 * h, 2 * h + 2))
                    if c == 7:
                        rms(c_l + 4, 2, BR, EPS4)
                    for k in Y_OUT.get(c - 1, ()):
                        split_hi(k, l * 32 + (16 + k + 1))
                    if c == 3:
                        glu_square(3)
                    if c == CH_HALF:
                        out_evac(0, 0)
                    if c == CH_HALF + 3:
                        out_store(0, 0, True)
                own.restart()

                def out_pair(i, more):
                    for c in range(CH_PAIR):
                        hi(n_l + N_OUT + i * CH_PAIR, c)
                        if c == 0:
                            out_evac(i - 1, 1)
                        if c == 3:
                            out_store(i - 1, 1, True)
                        if c == CH_HALF:
                            out_evac(i, 0)
                        if c == CH_HALF + 3:
                            out_store(i, 0, more)

                with act.Fori(1, 7) as i:
                    out_pair(i, True)
                out_pair(7, False)
                out_evac(7, 1)
                act.wait_ge(outx, l * 16 + 16)
                A(ssq[:, 0:2, :], zb[:, KT - 2:KT, :], ACT.Square).then_inc(last_squared, 1)
                out_store(7, 1, False)
            rms(4 * L + 1, 2, D, EPS1)

        @block.vector
        def _(dve):
            own = Own(dve, dve_own)
            V = nc.vector

            def lo(n0, c):
                s, d = (c + LOOK) % RAW, (c + LOOK) % W2
                dve.wait_ge(hi_ready, n0 + (c + LOOK + 1))
                V.tensor_tensor(w2[:, d, :, 1, :], raw[:, s, :, :], w2[:, d, :, 0, :].bitcast(F),
                                ALU.subtract).then_inc(w2_ready, 1)

            def evac(h0, half, dst, tiles=2):
                dve.wait_ge(lo_copied, h0 + 1)
                V.tensor_tensor(dst, half_lo[:, 0:tiles, :], ps[:, 2 * half:2 * half + tiles, T:],
                                ALU.add).then_inc(acc_read, 1)

            def reciprocals(count, cols):
                dve.wait_ge(rms_ready, count)
                V.reciprocal(rcol[:, 0:cols], ncol[:, 0:cols]).then_inc(rcol_ready, 1)

            def h_mul(c, n):
                if c >= 3:
                    dve.wait_ge(h_ready, n + (c - 2))
                for q in range(2):
                    k = 2 * c + q
                    last = V.scalar_tensor_tensor(out=hf[c % 3][:, q, :], in0=zb[:, k, :], scalar=sm[:, k:k + 1],
                                                  in1=ps[:, B_BU, 0:T], op0=ALU.mult, op1=ALU.mult)
                last.then_inc(hf_ready, 1)

            def y_mul(k, n):
                if k >= 3:
                    dve.wait_ge(h_ready, n + (k - 2))
                if k < 4:
                    src, r = zb[:, 2 * k:2 * k + 2, :], ps[:, B_BU, 0:T]
                elif k < 8:
                    q = k - 4
                    src = vb[:, 2 * q:2 * q + 2, :, :].rearrange("p g t d -> p g (t d)")
                    r = ps[:, B_A + q // 2, T * (q % 2):T * (q % 2) + T]
                elif k < 12:
                    src, r = ymla[:, 2 * k - 16:2 * k - 14, :], ps[:, B_BU, T:]
                else:
                    src, r = gs5[:, 2 * k - 24:2 * k - 22, :], ps[:, B_Y, 0:T]
                V.tensor_tensor(hf[k % 3][:, :, :], src, r.unsqueeze(1).to_broadcast([P, 2, T]),
                                ALU.mult).then_inc(hf_ready, 1)

            dve.sem_inc(acc_read, 2)
            dve.sem_inc(iter_done, 1)
            dve.sem_inc(st_ready, 1)
            dve.sem_inc(tab_used, 1)
            dve.sem_inc(bu_read, 1)
            dve.sem_inc(yl_ready, 1)
            C1 = 6.28125
            C2 = float(np.floor((2 * np.pi - C1) * 2.0 ** 21) / 2.0 ** 21)
            C3 = float(2 * np.pi - C1 - C2)
            dve.wait_ge(sm_loaded, 16)
            dve.wait_ge(pos_loaded, 16)
            own.chain(V.tensor_copy(ga[:, :], posi[:, :]))
            own.chain(V.tensor_scalar(ga[:, :], ga[:, :], sm_all[:, 0, S_INVF:S_INVF + 1], None, ALU.mult))
            own.chain(V.tensor_scalar(gb[:, :], ga[:, :], 1.0 / (2 * np.pi), MAGIC, ALU.mult, ALU.add))
            own.chain(V.tensor_scalar(gb[:, :], gb[:, :], -MAGIC, None, ALU.add))
            for part in (C1, C2, C3):
                own.chain(V.scalar_tensor_tensor(out=ga[:, :], in0=gb[:, :], scalar=-part, in1=ga[:, :],
                                                 op0=ALU.mult, op1=ALU.add))
            V.tensor_scalar(ga[:, :], ga[:, :], 3.1415925, -3.1415925, ALU.min, ALU.max).then_inc(rope_made, 1)
            dve.wait_ge(rope_made, 1)
            for i in range(8):
                part = (sx if i == 0 else ke if i % 2 else nf)[:, :] if i < 6 else ssq[:, i - 6, :]
                dve.wait_ge(squares_made, i + 1)
                if 3 <= i < 6:
                    dve.wait_ge(x_added, i - 2)
                V.tensor_reduce(part, gs5[:, 4 * (i % 2):4 * (i % 2) + 4, :].rearrange("p a t -> p t a"), AX.X,
                                ALU.add).then_inc(x_ready, 1)
            dve.wait_ge(x_ready, 8)
            dve.sem_inc(last_squared, 1)
            for s in range(LOOK):
                dve.wait_ge(hi_ready, s + 1)
                V.tensor_tensor(w2[:, s, :, 1, :], raw[:, s, :, :], w2[:, s, :, 0, :].bitcast(F),
                                ALU.subtract).then_inc(w2_ready, 1)
            dve.wait_ge(consts_made, 1)
            own.restart()

            with dve.Fori(0, L) as l:
                n_l, h_l, c_l = l * N_LAYER, l * H_LAYER, l * 4

                def lru_abs():
                    dve.wait_ge(small_loaded, 32)
                    lam = pgl[:, :, C_LAM]
                    own.do(V.tensor_copy(pgl[:, :, 0:NPG_IN], pg_all[:, l, :, :]))
                    own.do(V.tensor_copy(s5[:, 0:3, :], s5_all[:, l, :, :]))
                    own.chain(V.tensor_scalar(lru8[:, 5, :], sm[:, S_BGLU:S_BGLU + G8], 0.5, None, ALU.mult))
                    own.do(V.tensor_scalar(pgl[:, :, C_HBA:C_HBX + 1], pgl[:, :, C_BA:C_BX + 1], 0.5, None, ALU.mult))
                    own.do(V.tensor_scalar(lru8[:, 3, :], lam, -1.0, 0.0, ALU.mult, ALU.max))
                    own.chain(V.tensor_scalar(lru8[:, 2, :], lam, -1.0, None, ALU.mult))
                    V.tensor_tensor(lru8[:, 0, :], lru8[:, 2, :], lam, ALU.max).then_inc(pgl_dve, 1)

                def lru_softplus():
                    dve.wait_ge(pgl_act, 2 * l + 1)
                    e, z, z2, a = lru8[:, 1, :], lru8[:, 0, :], lru8[:, 2, :], lru8[:, 4, :]
                    own.chain(V.tensor_scalar(z, e, 2.0, None, ALU.add))
                    own.chain(V.reciprocal(z, z))
                    own.chain(V.tensor_tensor(z, z, e, ALU.mult))
                    own.chain(V.tensor_tensor(z2, z, z, ALU.mult))
                    own.chain(V.tensor_scalar(a, z2, 1.0 / 17, None, ALU.mult))
                    for k in range(15, 1, -2):
                        own.chain(V.scalar_tensor_tensor(out=a, in0=a, scalar=1.0 / k, in1=z2, op0=ALU.add, op1=ALU.mult))
                    own.chain(V.scalar_tensor_tensor(out=a, in0=a, scalar=1.0, in1=z, op0=ALU.add, op1=ALU.mult))
                    own.chain(V.scalar_tensor_tensor(out=a, in0=a, scalar=2.0, in1=lru8[:, 3, :], op0=ALU.mult,
                                                     op1=ALU.add))
                    own.do(V.tensor_scalar(pgl[:, :, C_NSP4], a, -4.0, None, ALU.mult))
                    V.tensor_scalar(pgl[:, :, C_SP2], a, 2.0, None, ALU.mult).then_inc(pgl_dve, 1)

                def rows(a, n=1):
                    return s5[:, a:a + n, :]

                def expm1_small(dst, src, tmp, n):
                    t, p, m = rows(src, n), rows(dst, n), rows(tmp, n)
                    own.chain(V.tensor_scalar(t, t, 1.0 / 1024, None, ALU.mult))
                    own.chain(V.tensor_scalar(p, t, 1.0 / 5, 1.0, ALU.mult, ALU.add))
                    for k in (4, 3, 2):
                        own.chain(V.tensor_tensor(m, p, t, ALU.mult))
                        own.chain(V.tensor_scalar(p, m, 1.0 / k, 1.0, ALU.mult, ALU.add))
                    own.chain(V.tensor_tensor(p, p, t, ALU.mult))

                def square_up(dst, n, times):
                    p = rows(dst, n)
                    for _ in range(times):
                        own.chain(V.scalar_tensor_tensor(out=p, in0=p, scalar=2.0, in1=p, op0=ALU.add, op1=ALU.mult))

                def s5_relu():
                    own.do(V.tensor_scalar(rows(3), rows(0), 0.0, None, ALU.max))
                    own.chain(V.tensor_scalar(rows(4), rows(0), -1.0, 0.0, ALU.mult, ALU.max))
                    expm1_small(10, 3, 12, 2)

                def s5_dt():
                    own.chain(V.tensor_scalar(rows(10, 2), rows(10, 2), 1.0, None, ALU.add))
                    own.chain(V.reciprocal(rows(11), rows(11)))
                    own.chain(V.tensor_tensor(rows(3), rows(10), rows(11), ALU.mult))
                    own.chain(V.tensor_tensor(rows(4), rows(1), rows(3), ALU.mult))

                def s5_turns():
                    own.chain(V.tensor_tensor(rows(6), rows(2), rows(3), ALU.mult))
                    own.chain(V.tensor_scalar(rows(6), rows(6), 1.0 / (2 * np.pi), None, ALU.mult))
                    own.chain(V.tensor_scalar(rows(7), rows(6), MAGIC, None, ALU.add))
                    own.chain(V.tensor_scalar(rows(7), rows(7), -MAGIC, None, ALU.add))
                    V.tensor_tensor(rows(7), rows(6), rows(7), ALU.subtract).then_inc(pgl_dve, 1)

                def pcol(c):
                    return pgl[:, :, c:c + 4]

                def s5_scale():
                    dve.wait_ge(pgl_act, 2 * l + 2)
                    own.do(V.tensor_scalar(rows(10), rows(5), 1.0, None, ALU.add))
                    own.chain(V.tensor_tensor(rows(11), rows(9), rows(9), ALU.mult))
                    own.chain(V.scalar_tensor_tensor(out=rows(11), in0=rows(11), scalar=-2.0, in1=rows(10),
                                                     op0=ALU.mult, op1=ALU.mult))
                    own.chain(V.tensor_tensor(rows(11), rows(11), rows(5), ALU.add))
                    own.chain(V.tensor_tensor(rows(12), rows(10), rows(8), ALU.mult))
                    own.chain(V.tensor_tensor(rows(13), rows(1), rows(1), ALU.mult))
                    own.chain(V.tensor_tensor(rows(14), rows(2), rows(2), ALU.mult))
                    own.chain(V.tensor_tensor(rows(13), rows(13), rows(14), ALU.add))
                    own.chain(V.reciprocal(rows(13), rows(13)))

                def s5_scale2():
                    own.do(V.tensor_tensor(rows(14), rows(11), rows(1), ALU.mult))
                    own.do(V.tensor_tensor(rows(15), rows(12), rows(2), ALU.mult))
                    own.do(V.tensor_tensor(rows(16), rows(11), rows(2), ALU.mult))
                    own.chain(V.tensor_tensor(rows(17), rows(12), rows(1), ALU.mult))
                    own.do(V.tensor_tensor(rows(14), rows(14), rows(15), ALU.add))
                    own.chain(V.tensor_tensor(rows(16), rows(16), rows(17), ALU.subtract))
                    view = lambda a: s5[:, a, :].rearrange("p (g j) -> p g j", j=4)
                    own.do(V.tensor_tensor(pcol(C_SR), view(14), view(13), ALU.mult))
                    own.do(V.tensor_tensor(pcol(C_NSI), view(16), view(13), ALU.mult))
                    own.do(V.tensor_copy(pcol(C_R), view(10)))
                    V.tensor_copy(pcol(C_F0), view(7)).then_inc(dve_prep, 1)

                def k_rotate():
                    dve.wait_ge(act_prep, 4)
                    dve.wait_ge(kperm_ready, l + 1)
                    V.tensor_tensor(qr[:, :], ps[:, B_A, 0:T], rope[:, :], ALU.mult).then_inc(krot_ready, 1)

                def k_keep():
                    dve.wait_ge(ksum_ready, l + 1)
                    V.tensor_copy(kext[:, :], ps[:, B_A, 0:T]).then_inc(kext_ready, 1)

                def latent(k):
                    if k == 0:
                        dve.wait_ge(rstd_ready, c_l + 2)
                    r = ps[:, B_B, 0:T] if k < CQ else ps[:, B_B, T:]
                    V.scalar_tensor_tensor(out=zb[:, Z_CQ + k, :], in0=zb[:, Z_CQ + k, :],
                                           scalar=sm[:, S_QG + k:S_QG + k + 1], in1=r, op0=ALU.mult,
                                           op1=ALU.mult).then_inc(latents_ready, 1)

                own.chain(V.tensor_copy(sm[:, :], sm_all[:, l, :]))
                reciprocals(c_l + 1, 2)
                dve.wait_ge(rstd_ready, c_l + 1)
                for c in range(3):
                    h_mul(c, l * 32)
                for c in range(CH_PAIR):
                    lo(n_l, c)
                    if c + 3 < CH_HALF:
                        h_mul(c + 3, l * 32)
                    if c == CH_HALF - 1:
                        dve.wait_ge(x_stored, 16 * (16 * l + 1))
                    if c % CH_HALF == CH_HALF - 1:
                        h = c // CH_HALF
                        evac(h_l + h, h, zb[:, 2 * h:2 * h + 2, :])
                own.restart()
                with dve.Fori(1, 8) as i:
                    for c in range(CH_PAIR):
                        lo(n_l + i * CH_PAIR, c)
                        if c % CH_HALF == CH_HALF - 1:
                            h = c // CH_HALF
                            evac(h_l + (i * 2 + h), h, zb[:, bass.ds(i * 4 + 2 * h, 2), :])
                for c in range(CH_PAIR):
                    lo(n_l + 8 * CH_PAIR, c)
                    if c == CH_HALF - 1:
                        evac(h_l + 16, 0, zb[:, KT:KT + 2, :])
                    if c == CH_PAIR - 1:
                        evac(h_l + 17, 1, kg[:, :].unsqueeze(1), 1)
                steps = {4: [k_rotate], 7: [k_keep], 9: [lru_abs], 11: [lru_softplus], 13: [s5_relu],
                         16: [lambda: square_up(10, 2, 5)], 18: [lambda: square_up(10, 2, 5)], 20: [s5_dt],
                         22: [lambda: reciprocals(c_l + 2, 4)], 24: [lambda: expm1_small(5, 4, 12, 1)],
                         26: [lambda: square_up(5, 1, 5)], 28: [lambda: square_up(5, 1, 5)], 30: [s5_turns],
                         36: [s5_scale], 38: [s5_scale2]}
                for k in range(CQ + CKV):
                    steps[40 + 2 * k] = [lambda k=k: latent(k)]
                for c in range(2 * CH_PAIR):
                    lo(n_l + N_V, c)
                    for step in steps.get(c, ()):
                        step()
                    if c % CH_HALF == CH_HALF - 1:
                        h = c // CH_HALF
                        evac(h_l + (H_V + h), h % 2, vb[:, 2 * h:2 * h + 2, :, :].rearrange("p g t d -> p t g d"))
                own.restart()

                with dve.Fori(0, G8) as g:
                    it = l * G8 + g
                    n0, h0 = n_l + N_GATE + g * CH_PAIR, h_l + H_GATE + g * 2

                    def s5_rotate(j):
                        dve.wait_ge(bu_ready, it * 4 + (j + 1))
                        dve.wait_ge(tab_ready, it * 4 + (j + 2))
                        dve.wait_ge(state_used, it * 4 + (j + 1))
                        own.do(V.tensor_tensor(xx[:, :, :], bu, tab[:, 0:1, :].to_broadcast([P, 2, T]), ALU.mult))

                    def s5_rotate2(j):
                        V.tensor_tensor(yy[:, :, :], bu[:, ::-1, :], tab[:, 2:0:-1, :], ALU.mult).then_inc(bu_read, 1)

                    def s5_sum(j):
                        own.wait()
                        dve.wait_ge(bu_read, it * 4 + (j + 2))
                        own.do(V.tensor_tensor(xx[:, :, :], xx[:, :, :], yy[:, :, :], ALU.add))

                    def s5_scan(j):
                        own.wait()
                        for a in range(2):
                            V.tensor_tensor_scan(g2[:, a, :], pg[:, C_R + j:C_R + j + 1].to_broadcast([P, T]),
                                                 xx[:, a, :], 0.0, ALU.mult, ALU.add).then_inc(scanned, 1)

                    def s5_back(j):
                        dve.wait_ge(scanned, it * 8 + (2 * j + 2))
                        V.tensor_tensor(yy[:, :, :], g2[:, ::-1, :], tab[:, 1:3, :], ALU.mult).then_inc(tab_used, 1)

                    def s5_state(j):
                        dve.wait_ge(tab_used, it * 4 + (j + 2))
                        dve.wait_ge(back_ready, it * 4 + (j + 2))
                        V.tensor_tensor(xx[:, :, :], xx[:, :, :], yy[:, :, :], ALU.add).then_inc(state_ready, 1)

                    def us_lo():
                        dve.wait_ge(us_ready, it * 2 + 2)
                        V.tensor_tensor(us[:, 1, :], zb[:, g + Z_S5, :], us[:, 0, :].bitcast(F),
                                        ALU.subtract).then_inc(us_split, 1)
                        V.tensor_tensor(blo[:, :, :], mixw[:, 2:4, :], bhi[:, :, :].bitcast(F),
                                        ALU.subtract).then_inc(us_split, 1)

                    def conv(d):
                        if d == 1:
                            dve.wait_ge(xc_begun, it + 1)
                        else:
                            own.wait()
                        last = V.scalar_tensor_tensor(out=xc[:, d:], in0=zb[:, g, 0:T - d],
                                                      scalar=pg[:, C_CONV + 3 - d:C_CONV + 4 - d], in1=xc[:, d:],
                                                      op0=ALU.mult, op1=ALU.add)
                        if d < 3:
                            own.do(last)
                        else:
                            last.then_inc(xc_ready, 1)

                    def lru_in():
                        dve.wait_ge(decays_ready, it + 1)
                        own.do(V.scalar_tensor_tensor(out=ke[:, :], in0=trti[:, 1, :], scalar=1.0, in1=xc[:, :],
                                                      op0=ALU.add, op1=ALU.mult))
                        own.do(V.scalar_tensor_tensor(out=sq[:, :], in0=decay[:, :], scalar=1.0, in1=sq[:, :],
                                                      op0=ALU.add, op1=ALU.mult))

                    def lru_in2():
                        own.wait()
                        own.do(V.scalar_tensor_tensor(out=ke[:, :], in0=ke[:, :], scalar=0.5, in1=sq[:, :],
                                                      op0=ALU.mult, op1=ALU.mult))

                    def lru_scan():
                        own.wait()
                        V.tensor_tensor_scan(yl[:, :], decay[:, :], ke[:, :], 0.0, ALU.mult, ALU.add).then_inc(yl_ready, 1)

                    def q_rotate():
                        dve.wait_ge(qn_ready, it + 1)
                        V.tensor_tensor(qr[:, :], ps[:, B_A, T:], rope[:, :], ALU.mult).then_inc(qr_ready, 1)

                    def row_max():
                        dve.wait_ge(sc_ready, it + 1)
                        own.pause()
                        own.do(V.tensor_tensor_reduce(prob[:, 0, :], ps[:, B_A, 0:P], kc[:, K_AMASK + P:K_AMASK + 2 * P], 1.0,
                                                      -3.0e38, ALU.add, ALU.max, row[:, 0:1]))
                        own.do(V.tensor_tensor_reduce(prob[:, 1:3, :].rearrange("p a t -> p (a t)"), ps[:, B_A, P:3 * P],
                                                      kc[:, K_AMASK:K_AMASK + 2 * P], 1.0, -3.0e38, ALU.add, ALU.max,
                                                      row[:, 1:2]))
                        own.wait()
                        V.tensor_scalar(row[:, 2:4], row[:, 0:2], -SCALE, None, ALU.mult).then_inc(max_ready, 1)

                    def prob_norm():
                        dve.wait_ge(prob_ready, it + 1)
                        own.chain(V.reciprocal(row[:, 6:8], row[:, 4:6]))
                        own.do(V.tensor_scalar(prob[:, 0, :], prob[:, 0, :], row[:, 6:7], None, ALU.mult))
                        own.wait()
                        V.tensor_scalar(prob[:, 1:3, :], prob[:, 1:3, :], row[:, 7:8], None,
                                        ALU.mult).then_inc(probn_ready, 1)

                    def gla_log():
                        dve.wait_ge(la_act, it + 1)
                        own.chain(V.tensor_scalar(qd[:, :], ps[:, B_B, 0:T], pg[:, C_GLAB:C_GLAB + 1], 0.0, ALU.add, ALU.min))
                        own.do(V.tensor_tensor(qd[:, :], qd[:, :], gb[:, :], ALU.subtract))

                    def gla_cum():
                        own.wait()
                        own.chain(V.tensor_tensor_scan(cum[:, :], kc[:, K_CMASK:K_CMASK + T], qd[:, :], 0.0, ALU.mult,
                                                       ALU.add))
                        V.tensor_scalar(tot[:, :], cum[:, 63::64], 1.0 / TAU, None, ALU.mult).then_inc(cum_ready, 1)

                    def gla_qk():
                        dve.wait_ge(gla_exp, it + 1)
                        dve.wait_ge(yl_ready, it + 2)
                        q, k = zb[:, g // 2 + Z_Q, :], zb[:, g // 2 + Z_K, :]
                        own.do(V.scalar_tensor_tensor(out=qd[:, :], in0=q, scalar=float(P) ** -0.5, in1=ep[:, :],
                                                      op0=ALU.mult, op1=ALU.mult))
                        own.do(V.tensor_tensor(ki[:, :], k, ga[:, :], ALU.mult))

                    def gla_k():
                        k = zb[:, g // 2 + Z_K, :]
                        own.wait()
                        V.tensor_tensor(ke[:, :], k, gb[:, :], ALU.mult).then_inc(qk_ready, 1)

                    def gla_mask():
                        dve.wait_ge(ket_copied, it + 1)
                        own.pause()
                        m = kc[:, K_GMASK:K_GMASK + P].bitcast(I).unsqueeze(1).to_broadcast([P, 2, P])
                        V.copy_predicated(attm[:, :, :], m, ps[:, B_A, 0:T].rearrange("p (b s) -> p b s", b=2))\
                            .then_inc(att_masked, 1)

                    def gla_state():
                        dve.wait_ge(kvs_ready, it * 2 + 2)
                        own.do(V.tensor_copy(st[:, 0, :], ps[:, B_B, 0:P]))

                    def gla_state2():
                        own.wait()
                        for c in (1, 2):
                            last = V.scalar_tensor_tensor(out=st[:, c, :], in0=st[:, c - 1, :],
                                                          scalar=ep[:, 64 * c + 63:64 * c + 64],
                                                          in1=ps[:, B_B, P * c:P * c + P], op0=ALU.mult, op1=ALU.add)
                            if c == 1:
                                own.chain(last)
                        last.then_inc(st_ready, 1)

                    bu = ps[:, B_BU, :].rearrange("p (a t) -> p a t", a=2)

                    def first_gates():
                        evac(h0, 0, gate[:, 0, :, :])

                    def gated(dst, y, c_gain, gt):
                        own.do(V.scalar_tensor_tensor(out=dst, in0=y[:, :], scalar=pg[:, c_gain:c_gain + 1], in1=gt,
                                                      op0=ALU.mult, op1=ALU.mult))

                    def lru_gated():
                        dve.wait_ge(silu_ready, it * 2 + 1)
                        dve.wait_ge(yl_squared, it + 1)
                        gated(zb[:, g, :], yl, C_LRUG, gate[:, 0, 0, :])

                    def mla_gated():
                        dve.wait_ge(ym_squared, it + 1)
                        gated(ymla[:, g, :], ym, C_MLAG, gate[:, 0, 1, :])

                    steps = {0: [us_lo, lambda: conv(1), lambda: conv(2)], 1: [lambda: conv(3)], 3: [q_rotate],
                             9: [row_max], 12: [lru_in, gla_log], 13: [gla_cum], 14: [prob_norm], 15: [lru_in2],
                             16: [lru_scan], 17: [gla_qk], 18: [gla_k], 19: [first_gates], 24: [gla_mask],
                             26: [gla_state], 27: [gla_state2], 29: [lru_gated], 30: [mla_gated]}
                    for j, at in enumerate((3, 10, 18, 24)):
                        for d, f in enumerate((s5_rotate, s5_rotate2, s5_sum, s5_scan, s5_back, s5_state)):
                            steps.setdefault(at + d, []).append(lambda f=f, j=j: f(j))
                    for c in range(CH_PAIR):
                        lo(n0, c)
                        if c == 0:
                            dve.wait_ge(pg_ready, it + 1)
                        for step in steps.get(c, ()):
                            step()
                    evac(h0 + 1, 1, gate[:, 1, :, :])
                    dve.wait_ge(state_used, it * 4 + 5)
                    own.do(V.scalar_tensor_tensor(out=zb[:, g + Z_S5, :], in0=zb[:, g + Z_S5, :], scalar=pg[:, C_S5D:C_S5D + 1],
                                                  in1=ps[:, B_Y, 0:T], op0=ALU.mult, op1=ALU.add))
                    dve.wait_ge(silu_ready, it * 2 + 2)
                    dve.wait_ge(yg_squared, it + 1)
                    gated(vb[:, g, :, :].rearrange("p t d -> p (t d)"), yg, C_GLAG, gate[:, 1, 0, :])
                    own.wait()
                    dve.sem_inc(iter_done, 1)
                    own.restart()

                for q in range(4):
                    dve.wait_ge(gelu_done, l * 4 + (q + 1))
                    V.tensor_tensor(hb[:, 24 + 2 * q:26 + 2 * q, 1, :], zb[:, Z_S5 + 2 * q:Z_S5 + 2 * q + 2, :],
                                    hb[:, 24 + 2 * q:26 + 2 * q, 0, :].bitcast(F), ALU.subtract).then_inc(glu_ready, 1)
                reciprocals(c_l + 3, 12)

                def glu_mul(m):
                    z = zb[:, Z_S5 + 2 * m:Z_S5 + 2 * m + 2, :]
                    dve.wait_ge(glu_tanh, l * 4 + (m + 1))
                    V.scalar_tensor_tensor(out=z, in0=gate[:, m % 2, :, :], scalar=1.0, in1=z, op0=ALU.add,
                                           op1=ALU.mult).then_inc(y2_ready, 1)

                def glu_gated(m):
                    dve.wait_ge(y2_ready, l * 4 + (m + 1))
                    for q in range(2):
                        k = 2 * m + q
                        own.do(V.scalar_tensor_tensor(out=gs5[:, k, :], in0=zb[:, Z_S5 + k, :],
                                                      scalar=sm[:, S_S5G + k:S_S5G + k + 1], in1=gs5[:, k, :],
                                                      op0=ALU.mult, op1=ALU.mult))

                for c in range(4 * CH_GLU):
                    lo(n_l + N_GLU, c)
                    if c == 3:
                        dve.wait_ge(rstd_ready, c_l + 3)
                    m = c // CH_GLU - 1
                    if m >= 0 and c % CH_GLU == 0:
                        evac(h_l + (H_GLU + m), m % 2, gate[:, m % 2, :, :])
                    if c in Y_GLU:
                        y_mul(Y_GLU[c], l * 32 + 16)
                    if m >= 0 and c % CH_GLU == 2:
                        glu_mul(m)
                    if m >= 0 and c % CH_GLU == 3:
                        glu_gated(m)

                def out_end(i, h):
                    z = zb[:, bass.ds(i * 4 + 2 * h, 2), :]
                    evac(h_l + H_OUT + (i * 2 + h), h, z)
                    dve.wait_ge(acc_read, h_l + H_OUT + (i * 2 + (h + 3)))
                    dve.wait_ge(xold_loaded[h], l * 128 + (i * 16 + 16))
                    V.tensor_tensor(z, z, gate[:, h, :, :], ALU.add).then_inc(outx, 1)

                for c in range(CH_PAIR):
                    if c == 7:
                        reciprocals(c_l + 4, 2)
                    lo(n_l + N_OUT, c)
                    if c == 0:
                        evac(h_l + (H_GLU + 3), 1, gate[:, 1, :, :])
                    if c == 2:
                        glu_mul(3)
                    if c == 3:
                        glu_gated(3)
                        own.wait()
                    if c == 10:
                        dve.wait_ge(rstd_ready, c_l + 4)
                    for k in Y_OUT.get(c, ()):
                        y_mul(k, l * 32 + 16)
                    if c == CH_HALF - 1:
                        dve.wait_ge(glu_squared, l * 4 + 4)
                    if c == CH_HALF:
                        out_end(0, 0)
                own.restart()
                with dve.Fori(1, 8) as i:
                    for c in range(CH_PAIR):
                        lo(n_l + N_OUT + i * CH_PAIR, c)
                        if c == 0:
                            out_end(i - 1, 1)
                        if c == CH_HALF:
                            out_end(i, 0)
                out_end(7, 1)

            reciprocals(4 * L + 1, 2)
            dve.wait_ge(rstd_ready, 4 * L + 1)
            dve.wait_ge(x_stored, 16 * (16 * L + 1))
            for k in range(KT):
                last = V.scalar_tensor_tensor(out=zb[:, k, :], in0=zb[:, k, :], scalar=sm[:, S_FG + k:S_FG + k + 1],
                                              in1=ps[:, B_BU, 0:T], op0=ALU.mult, op1=ALU.mult)
                if k % 8 == 7:
                    last.then_inc(outx_ready, 1)

        @block.gpsimd
        def _(pool):
            own = Own(pool, pool_own)
            G = nc.gpsimd
            own.do(G.memset(ones[:, :], 1.0))
            own.do(G.memset(cst[:, 0:1], EPS))
            own.do(G.memset(cst[:, 1:2], 4 * EPS))
            own.do(G.memset(cst[:, 2:3], float(np.pi / 2)))
            own.do(G.memset(cst[:, 3:4], 1.0))
            own.do(G.memset(attm[:, :, :], 0.0))
            own.wait()
            pool.sem_inc(consts_made, 1)
            for i in range(1, 6):
                pool.wait_ge(x_ready, i + 1)
                G.tensor_tensor(sx[:, :], sx[:, :], (ke if i % 2 else nf)[:, :], ALU.add).then_inc(x_added, 1)
                pool.wait_ge(x_added, i)
            pool.sem_inc(sx_ready, 1)
            pool.wait_ge(const_loaded, 16)
            own.restart()
            pool.sem_inc(back_ready, 1)

            def split_lo(k, count):
                pool.wait_ge(h_hi_ready, count)
                G.tensor_tensor(hb[:, 2 * k:2 * k + 2, 1, :], hf[k % 3][:, :, :],
                                hb[:, 2 * k:2 * k + 2, 0, :].bitcast(F), ALU.subtract).then_inc(h_ready, 1)

            def add_square(dst, src, done):
                own.chain(G.tensor_tensor(sx[:, :], src, src, ALU.mult))
                G.tensor_tensor(dst, dst, sx[:, :], ALU.add).then_inc(done, 1)

            with pool.Fori(0, L) as l:
                h_l, c_l = l * H_LAYER, l * 4
                for k in range(KT // 2):
                    split_lo(k, l * 32 + (k + 1))
                pool.wait_ge(acc_read, h_l + 16 + 3)
                for k in range(CQ + CKV):
                    dst, z = ssq[:, 2 if k < CQ else 3, :], zb[:, Z_CQ + k, :]
                    if k in (0, CQ):
                        G.tensor_tensor(dst, z, z, ALU.mult).then_inc(latent_squared, 1)
                    else:
                        add_square(dst, z, latent_squared)
                    pool.wait_ge(latent_squared, 10 * l + (k + 1))
                pool.wait_ge(cols_ready, c_l + 2)
                own.pause()
                own.chain(G.memset(ssq[:, :, :], 0.0))
                pool.wait_ge(dve_prep, l + 1)
                own.restart()
                with pool.Fori(0, G8) as g:
                    it = l * G8 + g
                    pool.wait_ge(iter_done, it + 1)
                    G.tensor_copy(pg[:, :], pgl[:, g, :]).then_inc(pg_ready, 1)
                    pool.wait_ge(pg_ready, it + 1)

                    def turns(j):
                        f0 = pg[:, C_F0 + j:C_F0 + j + 1]
                        iota = kc[:, K_IOTA:K_IOTA + T]
                        pool.wait_ge(tab_ready, it * 4 + (j + 1))
                        own.pause()
                        own.do(G.tensor_scalar(sx[:, :], iota, f0, None, ALU.mult))
                        own.chain(G.tensor_scalar(nf[:, :], iota, f0, MAGIC, ALU.mult, ALU.add))
                        own.chain(G.tensor_scalar(nf[:, :], nf[:, :], -MAGIC, None, ALU.add))
                        G.tensor_tensor(nf[:, :], nf[:, :], sx[:, :], ALU.subtract).then_inc(nf_ready, 1)
                        pool.wait_ge(nf_ready, it * 4 + (j + 1))

                    def back(j):
                        pool.wait_ge(scanned, it * 8 + (2 * j + 2))
                        G.tensor_tensor(xx[:, :, :], g2[:, :, :], tab[:, 0:1, :].to_broadcast([P, 2, T]),
                                        ALU.mult).then_inc(back_ready, 1)

                    turns(0)
                    pool.wait_ge(mix_loaded, it * 16 + 16)
                    pool.wait_ge(state_used, it * 4 + 1)
                    cr = mixw[:, 4, :].rearrange("p (j h) -> p j h", j=4)
                    ci = mixw[:, 5, :].rearrange("p (j h) -> p j h", j=4)
                    sr = pg[:, C_SR:C_SR + 4].unsqueeze(2).to_broadcast([P, 4, 32])
                    nsi = pg[:, C_NSI:C_NSI + 4].unsqueeze(2).to_broadcast([P, 4, 32])
                    t0 = sx[:, 0:P].rearrange("p (j h) -> p j h", j=4)
                    t1 = sx[:, P:T].rearrange("p (j h) -> p j h", j=4)
                    own.do(G.tensor_tensor(t0, cr, sr, ALU.mult))
                    own.chain(G.tensor_tensor(t1, ci, nsi, ALU.mult))
                    own.chain(G.tensor_tensor(cprime[:, 0, :, :], t0, t1, ALU.add))
                    own.do(G.tensor_tensor(t0, cr, nsi, ALU.mult))
                    own.chain(G.tensor_tensor(t1, ci, sr, ALU.mult))
                    G.tensor_tensor(cprime[:, 1, :, :], t0, t1, ALU.subtract).then_inc(cprime_ready, 1)
                    pool.wait_ge(cprime_ready, it + 1)
                    own.do(G.tensor_copy(vs[:, :, :], vb[:, g, :, :]))
                    own.wait()
                    pool.sem_inc(vs_ready, 1)
                    turns(1)
                    back(0)
                    turns(2)
                    back(1)
                    turns(3)
                    pool.wait_ge(yl_ready, it + 2)
                    add_square(ssq[:, 0, :], yl[:, :], yl_squared)
                    pool.wait_ge(yl_squared, it + 1)
                    pool.wait_ge(ym_ready, it + 2)
                    add_square(ssq[:, 1, :], ym[:, :], ym_squared)
                    pool.wait_ge(ym_squared, it + 1)
                    back(2)
                    back(3)
                    pool.wait_ge(yg_ready, it + 2)
                    add_square(ssq[:, g // 2 + 2, :], yg[:, :], yg_squared)
                    pool.wait_ge(yg_squared, it + 1)
                    own.restart()
                def add_pair(m):
                    pool.wait_ge(y2_squared, l * 4 + (m + 1))
                    a, b = ssq[:, 2 * (m % 2), :], ssq[:, 2 * (m % 2) + 1, :]
                    if m == 0:
                        G.tensor_tensor(sx[:, :], a, b, ALU.add).then_inc(glu_squared, 1)
                    else:
                        own.chain(G.tensor_tensor(sx[:, :], sx[:, :], a, ALU.add))
                        G.tensor_tensor(sx[:, :], sx[:, :], b, ALU.add).then_inc(glu_squared, 1)
                    pool.wait_ge(glu_squared, l * 4 + (m + 1))

                for c in range(4 * CH_GLU):
                    if c in Y_GLU:
                        split_lo(Y_GLU[c], l * 32 + (16 + Y_GLU[c] + 1))
                    if c >= CH_GLU and c % CH_GLU == 3:
                        add_pair(c // CH_GLU - 1)
                for c in range(CH_HALF):
                    for k in Y_OUT.get(c, ()):
                        split_lo(k, l * 32 + (16 + k + 1))
                    if c == 3:
                        add_pair(3)
                pool.wait_ge(cols_ready, c_l + 4)
                own.pause()
                own.chain(G.memset(sx[:, :], 0.0))
                own.restart()

                def out_squares(i, h):
                    pool.wait_ge(outx, l * 16 + (i * 2 + (h + 1)))
                    for q in range(2):
                        z = zb[:, i * 4 + (2 * h + q), :]
                        own.chain(G.tensor_tensor(nf[:, :], z, z, ALU.mult))
                        own.chain(G.tensor_tensor(sx[:, :], sx[:, :], nf[:, :], ALU.add))

                with pool.Fori(0, 7) as i:
                    for h in range(2):
                        out_squares(i, h)
                    own.restart()
                out_squares(7, 0)
                own.restart()
                pool.sem_inc(sx_ready, 1)


def _constants():
    c = np.zeros((P, NK), np.float32)
    r = np.arange(32)
    for a, b in ((0, 0), (1, 1), (2, 1), (3, 0)):
        c[32 * b + r, K_PERM1 + 32 * a + r] = 1
    for a in range(4):
        for b in ((0, 2), (1, 3))[a % 2]:
            c[32 * b + r, K_PERM2 + 32 * a + r] = 1
    c[:, K_ID:K_ID + P] = np.eye(P)
    i = np.arange(P)
    tri = np.where(i[None, :] <= i[:, None], 0.0, -HEAVY)
    c[:, K_AMASK + P:K_AMASK + 2 * P] = tri
    c[:, K_GMASK:K_GMASK + P] = (i[:, None] <= i[None, :]) & (i[:, None] // 64 == i[None, :] // 64)
    t = np.arange(T)
    c[:, K_CMASK:K_CMASK + T] = t % 64 != 0
    c[:, K_IOTA:K_IOTA + T] = t
    return c


def _columns(m, width):
    k, n = m.shape
    return m.reshape(k // (2 * P), 2, P, n // width, width).transpose(3, 0, 2, 1, 4)


def _weights(inp, l):
    w = inp["w_in"][l]
    at = np.cumsum([0, BR, BR, QR, KVR, ROPE, BR, 512, 512, BR, 16, BR, BR, BR])
    (s5u, s5g, cq, ckv, kr, mlag, gq, gk, gv, glr, glag, lruu, lrug) = [w[:, a:b] for a, b in zip(at[:-1], at[1:])]
    pad = np.zeros((D, 2 * CC - 256 - ROPE - 16), np.float32)
    tiles = lambda m: m.reshape(D, G8, 1, P)
    gates = np.concatenate([tiles(lrug), tiles(mlag), tiles(glag), tiles(s5g)], axis=2).reshape(D, 4 * BR)
    m = np.concatenate([lruu, s5u, gq, gk, cq, ckv, kr, glr, pad, gv, gates], axis=1)
    o = inp["w_out"][l]
    o = np.concatenate([o[3 * BR:], o[2 * BR:3 * BR], o[BR:2 * BR], o[:BR]], axis=0)
    parts = [_columns(m, CC), _columns(inp["s5_w_glu"][l], CC), _columns(o, CC)]
    return np.concatenate([p.reshape(-1, P, 2, CC) for p in parts])


def _tiles(v):
    return v.reshape(-1, P).T


def kernel(**inputs):
    import concourse.bacc as _bacc
    from concourse.bass_utils import run_bass_kernel_spmd as _run

    inp = {k: np.asarray(v) for k, v in inputs.items()}
    fp = np.float32
    arrays = {}
    arrays["w"] = np.concatenate([_weights(inp, l) for l in range(L)])
    arrays["x"] = np.ascontiguousarray(inp["x"][0].reshape(T, KT, P).transpose(2, 1, 0))
    arrays["pos"] = np.ascontiguousarray(inp["positions"])
    arrays["const"] = _constants()

    small = np.zeros((P, L, NS), fp)
    f = np.arange(32, dtype=fp) / fp(32)
    small[:, 0, S_INVF] = np.tile(fp(1) / fp(10000.0) ** f, 4)
    pg = np.zeros((P, L, G8, NPG_IN), fp)
    s5 = np.zeros((P, L, 3, 32), fp)
    mla = np.zeros((L * G8 + 1, P, CQ * T + 2 * KVR), fp)
    mix = np.zeros((L * G8 + 1, P, 6, P), fp)
    wg2 = np.zeros((L * G8 + 1, 16, P), fp)
    for l in range(L):
        g = lambda name: inp[name][l]
        for a, v in ((S_NORM, g("norm_g")), (S_QG, g("mla_q_norm_g")), (S_KVG, g("mla_kv_norm_g")),
                     (S_BGLU, g("s5_b_glu")), (S_S5G, g("s5_out_g")), (S_FG, inp["final_g"])):
            small[:, l, a:a + v.size // P] = _tiles(v)
        for j in range(4):
            pg[:, l, :, C_CONV + j] = _tiles(g("lru_conv_w")[j])
        for c, v in ((C_CONVB, "lru_conv_b"), (C_BA, "lru_b_a"), (C_BX, "lru_b_x"), (C_LAM, "lru_lambda"),
                     (C_LRUG, "lru_out_g"), (C_MLAG, "mla_out_g"), (C_GLAG, "gla_out_g")):
            pg[:, l, :, c] = _tiles(g(v))
        pg[:, l, :, C_S5D] = _tiles(g("s5_d").reshape(-1))
        for h in range(4):
            pg[:, l, 2 * h, C_GLAB] = pg[:, l, 2 * h + 1, C_GLAB] = g("gla_b_gate")[P * h:P * h + P]
        for a in range(2):
            r = slice(64 * a, 64 * a + 64)
            s5[r, l, 0, :] = g("s5_log_dt")[a::2][None, :]
            s5[r, l, 1, :] = g("s5_lambda_re")[a::2].T
            s5[r, l, 2, :] = g("s5_lambda_im")[a::2].T
        uq = g("mla_w_uq").reshape(CQ, P, G8, 128 + ROPE)
        uk, uv = g("mla_w_uk").reshape(CKV, P, G8, P), g("mla_w_uv").reshape(CKV, P, G8, P)
        for i in range(G8):
            n = l * G8 + i
            q = uq[:, :, i, :].transpose(1, 0, 2)
            q = np.concatenate([q, q[:, :, 160:192], q[:, :, 128:160]], axis=2)
            mla[n, :, 0:CQ * T] = q.reshape(P, CQ * T)
            mla[n, :, CQ * T:CQ * T + KVR] = uk[:, :, i, :].transpose(1, 0, 2).reshape(P, KVR)
            mla[n, :, CQ * T + KVR:] = uv[:, :, i, :].transpose(1, 0, 2).reshape(P, KVR)
            mix[n, :, 0], mix[n, :, 1] = g("lru_w_a")[i], g("lru_w_x")[i]
            wg2[n] = g("gla_w_gate")[:, P * (i // 2):P * (i // 2) + P]
            for j in range(4):
                for a in range(2):
                    grp = 8 * i + 2 * j + a
                    rows, states = slice(32 * j + 16 * a, 32 * j + 16 * a + 16), slice(64 * a, 64 * a + 64)
                    cols = slice(32 * j + 16 * a, 32 * j + 16 * a + 16)
                    mix[n, rows, 2, states] = g("s5_b_re")[grp].T
                    mix[n, rows, 3, states] = g("s5_b_im")[grp].T
                    mix[n, states, 4, cols] = g("s5_c_re")[grp].T
                    mix[n, states, 5, cols] = g("s5_c_im")[grp].T
    arrays.update(small=small, pg=pg, s5raw=s5, mlaw=mla, mixw=mix, wg2=wg2)

    nc = _bacc.Bacc("TRN2", target_bir_lowering=False, num_devices=1, dynamic_dma_scratch_size=1024)
    aps = {k: nc.dram_tensor(f"in_{k}", a.shape, mybir.dt.from_np(a.dtype), kind="ExternalInput").ap()
           for k, a in arrays.items()}
    out = nc.dram_tensor("out", (P, KT, T), mybir.dt.float32, kind="ExternalOutput").ap()
    trunk(nc, *(aps[k] for k in ("w", "x", "pos", "const", "small", "pg", "s5raw", "mlaw", "mixw", "wg2")), out)
    r = _run(nc, [{f"in_{k}": a for k, a in arrays.items()}], core_ids=[0])
    return r.results[0]["out"].transpose(2, 1, 0).reshape(1, T, D)
```
